# Optimizing a Trainium2 kernel written in Bass

```python
import math
import jax
import jax.numpy as jnp
from jax import lax
import numpy as np

D_MODEL = 4096
BATCH = 1
SEQ = 256
DEPTH = 1

HEAD_DIM = 128
N_SB_HEADS = 16
N_DIL_HEADS = 16
SB_WIDTH = N_SB_HEADS * HEAD_DIM
DIL_WIDTH = N_DIL_HEADS * HEAD_DIM
MIX_WIDTH = SB_WIDTH + DIL_WIDTH
SPLIT_SIZES = (SB_WIDTH, SB_WIDTH, SB_WIDTH, SB_WIDTH, DIL_WIDTH, DIL_WIDTH, DIL_WIDTH, DIL_WIDTH)
IN_COLS = sum(SPLIT_SIZES)
SPLIT_POINTS = tuple(sum(SPLIT_SIZES[:i + 1]) for i in range(len(SPLIT_SIZES) - 1))
Q_BLOCK = 128
DIL_PAIRS = ((128, 1), (512, 4), (2048, 16))
ALIBI_MAX_BIAS = 8.0
EPS = 1e-6

kernel_name = 'hybrid_stickbreak_dilated_block'

def rmsnorm(x, g):
    xf = x.astype(jnp.float32)
    y = xf * lax.rsqrt(jnp.mean(xf * xf, axis=-1, keepdims=True) + EPS)
    return (y * g.astype(jnp.float32)).astype(x.dtype)

def split_heads(t, n_heads):
    b, s, _ = t.shape
    return t.reshape(b, s, n_heads, HEAD_DIM).transpose(0, 2, 1, 3)

def head_rmsnorm_merge(y, g):
    b, h, s, d = y.shape
    yf = y.astype(jnp.float32)
    yf = yf * lax.rsqrt(jnp.mean(yf * yf, axis=-1, keepdims=True) + EPS)
    return yf.transpose(0, 2, 1, 3).reshape(b, s, h * d) * g.astype(jnp.float32)

def alibi_slopes(n_heads):
    return jnp.exp2(-ALIBI_MAX_BIAS * jnp.arange(1, n_heads + 1, dtype=jnp.float32) / n_heads)

def stick_breaking_attention(q, k, v):
    b, h, s, d = q.shape
    nb = s // Q_BLOCK
    inv_sqrt_d = 1.0 / math.sqrt(d)
    kf = k.astype(jnp.float32)
    vf = v.astype(jnp.float32)
    qb = q.astype(jnp.float32).reshape(b, h, nb, Q_BLOCK, d).transpose(2, 0, 1, 3, 4)
    k_pos = jnp.arange(s)

    def one_block(args):
        qi, blk = args
        z = jnp.einsum('bhqd,bhkd->bhqk', qi, kf) * inv_sqrt_d
        q_pos = blk * Q_BLOCK + jnp.arange(Q_BLOCK)
        mask = k_pos[None, :] < q_pos[:, None]
        log_beta = jax.nn.log_sigmoid(z)
        log_one_minus = jnp.where(mask, jax.nn.log_sigmoid(-z), 0.0)
        suffix = lax.cumsum(log_one_minus, axis=3, reverse=True) - log_one_minus
        a = jnp.where(mask, jnp.exp(log_beta + suffix), 0.0)
        return jnp.einsum('bhqk,bhkd->bhqd', a, vf)

    out = lax.map(one_block, (qb, jnp.arange(nb)))
    return out.transpose(1, 2, 0, 3, 4).reshape(b, h, s, d)

def dilated_branch(q, k, v, slopes, window, dilation):
    b, h, s, d = q.shape
    n = window // dilation
    L = s // dilation
    Lp = -(-L // n) * n
    nb = Lp // n
    inv_sqrt_d = 1.0 / math.sqrt(d)

    def to_local(t):
        t = t.astype(jnp.float32).reshape(b, h, L, dilation, d).transpose(0, 1, 3, 2, 4)
        t = jnp.pad(t, ((0, 0), (0, 0), (0, 0), (0, Lp - L), (0, 0)))
        return t.reshape(b, h, dilation, nb, n, d)

    def with_prev(t):
        prev = jnp.pad(t, ((0, 0), (0, 0), (0, 0), (1, 0), (0, 0), (0, 0)))[:, :, :, :-1]
        return jnp.concatenate([prev, t], axis=4)

    ql = to_local(q)
    kw = with_prev(to_local(k))
    vw = with_prev(to_local(v))
    qi = jnp.arange(n)[:, None]
    ki = jnp.arange(2 * n)[None, :] - n
    steps = qi - ki
    blk = jnp.arange(nb)[:, None, None]
    valid = (steps >= 0)[None] & (steps <= n)[None] & ((blk * n + ki[None]) >= 0)
    dist = (steps * dilation).astype(jnp.float32)
    sc = jnp.einsum('bhrnqd,bhrnkd->bhrnqk', ql, kw) * inv_sqrt_d
    sc = sc - slopes[None, :, None, None, None, None] * dist
    sc = jnp.where(valid, sc, -jnp.inf)
    m = jnp.max(sc, axis=-1, keepdims=True)
    p = jnp.exp(sc - m)
    den = jnp.sum(p, axis=-1, keepdims=True)
    num = jnp.einsum('bhrnqk,bhrnkd->bhrnqd', p, vw)

    def from_local(t):
        x_dim = t.shape[-1]
        t = t.reshape(b, h, dilation, Lp, x_dim)[:, :, :, :L]
        return t.transpose(0, 1, 3, 2, 4).reshape(b, h, s, x_dim)

    return from_local(num), from_local(den), from_local(m)

def dilated_attention(q, k, v):
    slopes = alibi_slopes(q.shape[1])
    parts = [dilated_branch(q, k, v, slopes, w, r) for (w, r) in DIL_PAIRS]
    m_all = parts[0][2]
    for part in parts[1:]:
        m_all = jnp.maximum(m_all, part[2])
    num = sum(pn * jnp.exp(pm - m_all) for (pn, _, pm) in parts)
    den = sum(pd * jnp.exp(pm - m_all) for (_, pd, pm) in parts)
    return num / den

def setup_inputs(seed: int = 0) -> dict:
    key = jax.random.key(seed)
    ks = jax.random.split(key, 10)
    x = jax.random.normal(ks[0], (BATCH, SEQ, D_MODEL), jnp.float32)
    c = jax.random.normal(ks[1], (BATCH, D_MODEL), jnp.float32)
    w_ada = jax.random.normal(ks[2], (DEPTH, D_MODEL, 3 * D_MODEL), jnp.float32) * D_MODEL ** -0.5
    b_ada = 0.01 * jax.random.normal(ks[3], (DEPTH, 3 * D_MODEL), jnp.float32)
    g_norm = 1.0 + 0.1 * jax.random.normal(ks[4], (DEPTH, D_MODEL), jnp.float32)
    w_in = jax.random.normal(ks[5], (DEPTH, D_MODEL, IN_COLS), jnp.float32) * D_MODEL ** -0.5
    g_sb = 1.0 + 0.1 * jax.random.normal(ks[6], (DEPTH, SB_WIDTH), jnp.float32)
    g_dil = 1.0 + 0.1 * jax.random.normal(ks[7], (DEPTH, DIL_WIDTH), jnp.float32)
    w_out = jax.random.normal(ks[8], (DEPTH, MIX_WIDTH, D_MODEL), jnp.float32) * MIX_WIDTH ** -0.5
    g_final = 1.0 + 0.1 * jax.random.normal(ks[9], (D_MODEL,), jnp.float32)
    return {'x': x, 'c': c, 'w_ada': w_ada, 'b_ada': b_ada, 'g_norm': g_norm,
            'w_in': w_in, 'g_sb': g_sb, 'g_dil': g_dil, 'w_out': w_out, 'g_final': g_final}

def reference(x, c, w_ada, b_ada, g_norm, w_in, g_sb, g_dil, w_out, g_final):
    cs = jax.nn.silu(c.astype(jnp.float32))
    for layer in range(DEPTH):
        mod = cs @ w_ada[layer].astype(jnp.float32) + b_ada[layer].astype(jnp.float32)
        shift, scale, gate = jnp.split(mod, 3, axis=-1)
        h = rmsnorm(x, g_norm[layer]).astype(jnp.float32) * (1.0 + scale[:, None, :]) + shift[:, None, :]
        proj = jnp.einsum('bsd,de->bse', h.astype(x.dtype), w_in[layer])
        sb_q, sb_k, sb_v, sb_z, dl_q, dl_k, dl_v, dl_z = jnp.split(proj, SPLIT_POINTS, axis=-1)
        y_sb = stick_breaking_attention(split_heads(sb_q, N_SB_HEADS), split_heads(sb_k, N_SB_HEADS),
                                        split_heads(sb_v, N_SB_HEADS))
        y_sb = head_rmsnorm_merge(y_sb, g_sb[layer]) * jax.nn.silu(sb_z.astype(jnp.float32))
        y_dl = dilated_attention(split_heads(dl_q, N_DIL_HEADS), split_heads(dl_k, N_DIL_HEADS),
                                 split_heads(dl_v, N_DIL_HEADS))
        y_dl = head_rmsnorm_merge(y_dl, g_dil[layer]) * jax.nn.silu(dl_z.astype(jnp.float32))
        y = jnp.concatenate([y_sb, y_dl], axis=-1).astype(x.dtype)
        out = jnp.einsum('bse,ed->bsd', y, w_out[layer])
        x = x + (gate[:, None, :] * out.astype(jnp.float32)).astype(x.dtype)
    return rmsnorm(x, g_final)


_drawn_inputs = setup_inputs


def setup_inputs(seed=0):
    import zlib

    import numpy as np

    out = dict(_drawn_inputs(seed))
    spreads = {}
    factors = {'b_ada': 4.867}
    for name, (base, spread) in spreads.items():
        noise = np.random.default_rng([zlib.crc32(name.encode()), seed]).standard_normal(out[name].shape)
        drawn = base * np.exp(spread * noise) if base else spread * noise
        out[name] = jnp.asarray(drawn.astype(out[name].dtype))
    for name, factor in factors.items():
        out[name] = (out[name] * factor).astype(out[name].dtype)
    return out
```

```python
from contextlib import ExitStack

import numpy as np
import concourse.bass as bass
from concourse import mybir

F32 = mybir.dt.float32
F32R = mybir.dt.float32r
BF16 = mybir.dt.bfloat16
I32 = mybir.dt.int32
ALU = mybir.AluOpType
ACT = mybir.ActivationFunctionType
AX = mybir.AxisListType

P = 128
S = 256
SB = S // P
D = 4096
KC = D // P
HEADS = 32
SB_HEADS = 16
HG = 4
GW = HG * P
GROUPS = HEADS // HG
SB_GROUPS = SB_HEADS // HG
UNITS = 4
TK = 4
TPU = KC // TK
TILE = TK * GW
RING = 4
ENTRIES = TPU + 2
ADA_ENTRIES = 2 * 2 * KC
OUT_UNITS = D // GW
PROJ_BASE = ADA_ENTRIES
OUT_BASE = PROJ_BASE + GROUPS * UNITS * ENTRIES
KEYS = 3 * P
VW = P + 1
EPS = 1e-6
INV_SQRT_D = float(P) ** -0.5
SLOPES = [2.0 ** (-8.0 * (h + 1) / (HEADS - SB_HEADS)) for h in range(HEADS - SB_HEADS)]
MASKED = -1.0e30
WINDOW = 128
ACC_PER_GROUP = 2 * HG + 2 * SB
ACC_AT = [0, HG, 2 * HG, 2 * HG + SB]
OUT_ACC = GROUPS * ACC_PER_GROUP
MASK_STEPS = 14


def build(nc, x, c, w_ada, b_ada, g_norm, w_in, g_sb, g_dil, w_out, g_final, out):
    x_rows = x.rearrange("o (s p) d -> p (o s) d", p=P)
    out_rows = out.rearrange("o (s p) d -> p (o s) d", p=P)
    ada_rows = w_ada.rearrange("l (k p) e -> (l k) p e", p=P)
    in_tiles = w_in.rearrange("l (t k p) e -> (l t) p k e", p=P, k=TK)
    out_tiles = w_out.rearrange("l (t k p) e -> (l t) p k e", p=P, k=TK)

    with ExitStack() as ctx:
        def sb(name, shape, dt=F32):
            return ctx.enter_context(nc.sbuf_tensor(name, shape, dt))

        def sem(name):
            return ctx.enter_context(nc.semaphore(name))

        act_split = sb("act_split", [P, KC, 2 * S], F32R)
        act_t = sb("act_t", [P, KC, S])
        xnew = act_t[:, :, :].rearrange("p k s -> p (k s)").rearrange("p (s d) -> p s d", s=SB)
        ring = sb("ring", [P, RING, TILE])
        w_hi = sb("w_hi", [P, 2, TK, GW], F32R)
        w_lo = sb("w_lo", [P, 2, TK, GW], F32R)
        ada_acc = sb("ada_acc", [P, D])
        heads_in = sb("heads_in", [P, 4, HG * S])
        shift_acc = heads_in[:, :, :].rearrange("p a b -> p (a b)")
        q_t = heads_in[:, 0, :].rearrange("p (j s) -> p j s", j=HG)
        k_t = heads_in[:, 1, :].rearrange("p (j s) -> p j s", j=HG)
        z_gate = heads_in[:, 2, :].rearrange("p (s e) -> p s e", s=SB)
        y_nat = heads_in[:, 3, :].rearrange("p (j s d) -> p j s d", j=HG, s=SB)
        gate_row = heads_in[:, 0, :].rearrange("p (a e) -> p a e", a=2)
        res = heads_in[:, 1, :].rearrange("p (s e) -> p s e", s=SB)
        v_ones = sb("v_ones", [P, SB, HG, VW])
        attn = sb("attn", [P, 2 * HG * KEYS + 2 * KEYS + 2 * (KEYS + 2)])
        probs = attn[:, 0:HG * KEYS].rearrange("p (j c) -> p j c", j=HG)
        probs_t = attn[:, HG * KEYS:2 * HG * KEYS].rearrange("p (j c) -> p j c", j=HG)
        at = 2 * HG * KEYS
        keep = attn[:, at:at + 2 * KEYS].rearrange("p (a c) -> p a c", a=2)
        at += 2 * KEYS
        left = attn[:, at:at + 2 * (KEYS + 2)].rearrange("p (a c) -> p a c", a=2)
        x_half = attn[:, 0:D]
        pos_t = attn[:, 0:KEYS].bitcast(I32)
        pos_n = attn[:, KEYS:2 * KEYS].bitcast(I32)
        tmp = [attn[:, (2 + i) * KEYS:(3 + i) * KEYS] for i in range(6)]
        g_final_row = sb("g_final_row", [P, GW])
        ident = sb("ident", [P, P])
        diag = sb("diag", [P, P])
        ones = sb("ones", [P, P])
        stop_mask = sb("stop_mask", [P, KEYS], BF16)
        dist_mask = sb("dist_mask", [P, KEYS], BF16)
        causal_t = sb("causal_t", [P, KEYS], BF16)
        count_t = sb("count_t", [P, KEYS], BF16)
        vec_rows = sb("vec_rows", [3 * KC, P])
        vec_t = sb("vec_t", [P, 3 * KC])
        c_t = sb("c_t", [P, KC])
        mul_t = sb("mul_t", [P, KC])
        add_t = sb("add_t", [P, KC])
        slope = sb("slope", [P, len(SLOPES)])
        neg_max = sb("neg_max", [P, HG, SB])
        sums = sb("sums", [P, HG, SB])
        dens = sb("dens", [P, HG, SB])
        den_sq = sb("den_sq", [P, HG, SB])
        rstd = sb("rstd", [P, HG, SB])
        minus_half = sb("minus_half", [P, HG, SB])
        x_sum = sb("x_sum", [P, SB])
        out_sums = sb("out_sums", [P, SB, OUT_UNITS])
        out_sum = sb("out_sum", [P, SB])
        out_rstd = sb("out_rstd", [P, SB])

        acc = ctx.enter_context(nc.psum_tensor("acc", [P, 4, 512], F32))
        att = ctx.enter_context(nc.psum_tensor("att", [P, 4, 512], F32))

        raw_ready = [sem(f"raw_ready{i}") for i in range(RING)]
        ring_used = sem("ring_used")
        hi_ready = sem("hi_ready")
        tile_done = sem("tile_done")
        acc_done = sem("acc_done")
        cross_ready = sem("cross_ready")
        sigma_ready = sem("sigma_ready")
        acc_taken = sem("acc_taken")
        vec_ready = sem("vec_ready")
        seed_ready = sem("seed_ready")
        gate_seeded = sem("gate_seeded")
        x_ready = sem("x_ready")
        ident_ready = sem("ident_ready")
        zeroed = sem("zeroed")
        pos_ready = sem("pos_ready")
        mask_step = sem("mask_step")
        vec_turned = sem("vec_turned")
        vec_copied = sem("vec_copied")
        c_sigma = sem("c_sigma")
        c_ready = sem("c_ready")
        x_squared = sem("x_squared")
        x_stat = sem("x_stat")
        x_turned = sem("x_turned")
        x_copied = sem("x_copied")
        mod_summed = sem("mod_summed")
        mod_ready = sem("mod_ready")
        h_ready = sem("h_ready")
        split_hi = sem("split_hi")
        split_lo = sem("split_lo")
        ones_set = sem("ones_set")
        scores_ready = sem("scores_ready")
        keep_ready = sem("keep_ready")
        left_ready = sem("left_ready")
        probs_a = sem("probs_a")
        biased = sem("biased")
        max_ready = sem("max_ready")
        probs_b = sem("probs_b")
        probs_turned = sem("probs_turned")
        probs_t_ready = sem("probs_t_ready")
        y_ready = sem("y_ready")
        y_squared = sem("y_squared")
        den_step = sem("den_step")
        var_ready = sem("var_ready")
        rstd_ready = sem("rstd_ready")
        y_normed = sem("y_normed")
        y_turned = sem("y_turned")
        y_taken = sem("y_taken")
        gate_ready = sem("gate_ready")
        gate_copied = sem("gate_copied")
        xg_ready = sem("xg_ready")
        res_ready = sem("res_ready")
        gained = sem("gained")
        res_squared = sem("res_squared")
        tail_step = sem("tail_step")
        out_rstd_ready = sem("out_rstd_ready")
        scaled_v = sem("scaled_v")
        scaled_s = sem("scaled_s")
        out_done = sem("out_done")

        def acc_before(g, t):
            return g * ACC_PER_GROUP + ACC_AT[t]

        def entry_slot(g, t, e):
            return (t * ENTRIES + e) % RING

        def entry_wait(eng, g, t, e):
            n = t * ENTRIES + e
            eng.wait_ge(raw_ready[n % RING], g * (16 * UNITS * ENTRIES // RING) + 16 * (PROJ_BASE // RING + n // RING + 1))

        def out_entry_wait(eng, v, e):
            eng.wait_ge(raw_ready[e % RING], v * (16 * TPU // RING) + 16 * (OUT_BASE // RING + e // RING + 1))

        def weight_entry(t):
            return t if t < TPU // 2 else t + 1

        block = ctx.enter_context(nc.Block())

        @block.sync
        def _(sp):
            def ada(dst_slot, k, half, third):
                lo = third * D + half * (D // 2)
                sp.dma_start(ring[:, dst_slot, :], ada_rows[k, :, lo:lo + D // 2]).then_inc(raw_ready[dst_slot], 16)

            for n in range(RING):
                ada(n, n // 2, n % 2, 1)
            with sp.Fori(1, KC // 2) as i:
                for n in range(RING):
                    sp.wait_ge(ring_used, i * RING + n - RING + 1)
                    ada(n, i * 2 + n // 2, n % 2, 1)
            with sp.Fori(0, KC // 2) as i:
                for n in range(RING):
                    sp.wait_ge(ring_used, i * RING + 2 * KC + n - RING + 1)
                    ada(n, i * 2 + n // 2, n % 2, 0)
            with sp.Fori(0, 2) as part:
                with sp.Fori(0, SB_GROUPS) as gg:
                    for t in range(UNITS):
                        for e in range(ENTRIES):
                            slot = entry_slot(0, t, e)
                            sp.wait_ge(ring_used, (part * SB_GROUPS + gg) * (UNITS * ENTRIES)
                                       + PROJ_BASE + t * ENTRIES + e - RING + 1)
                            if e == TPU // 2 or e == ENTRIES - 1:
                                half = 0 if e == TPU // 2 else 1
                                ada(slot, (part * SB_GROUPS + gg) * UNITS + t, half, 2)
                                continue
                            tile = e if e < TPU // 2 else e - 1
                            col = part * (UNITS * SB_HEADS * P) + gg * GW + t * SB_HEADS * P
                            sp.dma_start(ring[:, slot, :].rearrange("p (k e) -> p k e", k=TK),
                                         in_tiles[tile, :, :, bass.ds(col, GW)]).then_inc(raw_ready[slot], 16)

            def out_piece(v):
                sp.dma_start(g_final_row[:, :], g_final[bass.ds(v * GW, GW)].rearrange("(o e) -> o e", o=1)
                             .to_broadcast([P, GW])).then_inc(xg_ready, 16)
                sp.wait_ge(split_lo, 2 * TPU)
                sp.dma_start(xnew[:, :, bass.ds(v * GW, GW)], x_rows[:, :, bass.ds(v * GW, GW)]).then_inc(xg_ready, 16)

            def out_unit(v, first=False):
                for e in range(TPU):
                    sp.wait_ge(ring_used, v * TPU + OUT_BASE + e - RING + 1)
                    sp.dma_start(ring[:, e % RING, :].rearrange("p (k e) -> p k e", k=TK),
                                 out_tiles[e, :, :, bass.ds(v * GW, GW)]).then_inc(raw_ready[e % RING], 16)
                    if e == 0 and not first:
                        if not isinstance(v, int) or v > 1:
                            sp.wait_ge(gained, v * SB - SB)
                        out_piece(v - 1)

            out_unit(0, first=True)
            out_unit(1)
            with sp.Fori(1, OUT_UNITS // 2) as i:
                out_unit(i * 2)
                out_unit(i * 2 + 1)
            sp.wait_ge(gained, (OUT_UNITS - 1) * SB)
            out_piece(OUT_UNITS - 1)
            for n in range(2):
                sp.wait_ge(scaled_v, n + 1)
                sp.dma_start(out_rows[:, 0, n * D // 2:(n + 1) * D // 2], xnew[:, 0, n * D // 2:(n + 1) * D // 2]).then_inc(out_done, 16)
                sp.wait_ge(scaled_s, n + 1)
                sp.dma_start(out_rows[:, 1, n * D // 2:(n + 1) * D // 2], xnew[:, 1, n * D // 2:(n + 1) * D // 2]).then_inc(out_done, 16)
            sp.wait_ge(out_done, 64)

        @block.gpsimd
        def _(pool):
            pool.memset(ident[:, :], 0.0).then_inc(ident_ready, 1)
            pool.wait_ge(ident_ready, 1)
            pool.affine_select(out=ident[:, :], in_=ident[:, :], compare_op=ALU.not_equal, fill=1.0, base=0,
                               pattern=[[-1, P]], channel_multiplier=1).then_inc(ident_ready, 1)
            for a, dq in ((0, 0), (1, P), (2, 0)):
                pool.iota(pos_t[:, a * P:(a + 1) * P], pattern=[[1, P]], base=dq, channel_multiplier=-1)
                pool.iota(pos_n[:, a * P:(a + 1) * P], pattern=[[-1, P]], base=dq, channel_multiplier=1).then_inc(pos_ready, 1)
            pool.memset(ada_acc[:, :], 0.0).then_inc(zeroed, 1)
            pool.memset(shift_acc, 0.0).then_inc(zeroed, 1)
            pool.memset(ones[:, :], 1.0)
            for h, s in enumerate(SLOPES):
                pool.memset(slope[:, h:h + 1], s)
            pool.memset(minus_half[:, :, :], -0.5).then_inc(ident_ready, 1)
            pool.wait_ge(ident_ready, 3)
            for s in range(SB):
                pool.wait_ge(x_squared, s + 1)
                pool.tensor_scalar(x_sum[:, s:s + 1], x_sum[:, s:s + 1], 1.0 / D, EPS, ALU.mult, ALU.add).then_inc(x_stat, 1)
                pool.wait_ge(x_stat, 3 * s + 1)
                pool.tensor_tensor(x_sum[:, s:s + 1], x_sum[:, s:s + 1], minus_half[:, 0, 0:1], ALU.pow).then_inc(x_stat, 1)
                pool.wait_ge(x_stat, 3 * s + 2)
                if s:
                    pool.wait_ge(x_turned, TPU)
                pool.tensor_scalar(diag[:, :], ident[:, :], x_sum[:, s:s + 1], None, ALU.mult).then_inc(x_stat, 1)
            pool.wait_ge(mod_summed, 1)
            pool.memset(ada_acc[:, :], 0.0).then_inc(zeroed, 1)
            pool.wait_ge(x_turned, 2 * TPU)
            pool.memset(v_ones[:, :, :, P:VW], 1.0)
            pool.memset(left[:, :, P:P + 1], 1.0)
            pool.memset(left[:, :, KEYS + 1:KEYS + 2], 1.0).then_inc(ones_set, 1)
            with pool.Fori(0, GROUPS) as g:
                pool.wait_ge(var_ready, g + 1)
                pool.tensor_tensor(rstd[:, :, :], sums[:, :, :], minus_half[:, :, :], ALU.pow).then_inc(rstd_ready, 1)
            pool.wait_ge(tail_step, 2)
            pool.tensor_tensor(out_rstd[:, :], out_sum[:, :], minus_half[:, 0, :], ALU.pow).then_inc(out_rstd_ready, 1)

        @block.scalar
        def _(act):
            act.dma_start(vec_rows[0:KC, :], c.rearrange("o (k p) -> (o k) p", p=P)).then_inc(vec_ready, 16)
            act.dma_start(vec_rows[KC:2 * KC, :], g_norm.rearrange("l (k p) -> (l k) p", p=P)).then_inc(vec_ready, 16)
            act.dma_start(vec_rows[2 * KC:2 * KC + SB_HEADS, :], g_sb.rearrange("l (k p) -> (l k) p", p=P)).then_inc(vec_ready, 16)
            act.dma_start(vec_rows[2 * KC + SB_HEADS:3 * KC, :], g_dil.rearrange("l (k p) -> (l k) p", p=P)).then_inc(vec_ready, 16)
            act.wait_ge(zeroed, 2)
            act.dma_start(ada_acc[0:1, :], b_ada[:, D:2 * D]).then_inc(seed_ready, 16)
            act.dma_start(shift_acc[0:1, :], b_ada[:, 0:D]).then_inc(seed_ready, 16)
            act.wait_ge(mask_step, MASK_STEPS)
            act.dma_start(x_half, x_rows[:, 0, :]).then_inc(x_ready, 16)
            act.wait_ge(vec_copied, 1)
            act.activation(c_t[:, :], vec_t[:, 0:KC], ACT.Sigmoid).then_inc(c_sigma, 1)
            for s in range(SB):
                act.wait_ge(x_ready, 16 * (s + 1))
                act.activation(act_t[:, :, s * P:(s + 1) * P], x_half.rearrange("p (k e) -> p k e", k=KC), ACT.Square,
                               accum_out=x_sum[:, s:s + 1]).then_inc(x_squared, 1)
                act.wait_ge(x_squared, s + 1)
                for b in range(TPU):
                    act.wait_ge(x_turned, s * TPU + b + 1)
                    act.activation(act_t[:, b * TK:(b + 1) * TK, s * P:(s + 1) * P],
                                   acc[:, b % 4, :].rearrange("p (k e) -> p k e", k=TK), ACT.Copy).then_inc(x_copied, 1)
                if s == 0:
                    act.dma_start(x_half, x_rows[:, 1, :]).then_inc(x_ready, 16)
            act.wait_ge(zeroed, 3)
            act.dma_start(ada_acc[0:1, :], b_ada[:, 2 * D:3 * D]).then_inc(gate_seeded, 16)

            def hi(slot, m, m1):
                act.activation(w_hi[:, m1, :, :].rearrange("p k e -> p (k e)"), ring[:, slot, :], ACT.Copy).then_inc(hi_ready, 1)

            def split(g, t, i):
                first = isinstance(g, int) and g == 0 and t == 0
                if i >= 2:
                    act.wait_ge(tile_done, g * (UNITS * (TPU - 1)) + t * (TPU - 1) + i - 1)
                elif i == 0 and not first:
                    act.wait_ge(tile_done, g * (UNITS * (TPU - 1)) + t * (TPU - 1))
                elif i == 1 and not first:
                    act.wait_ge(acc_done, acc_before(g, t))
                entry_wait(act, g, t, weight_entry(i))
                hi(entry_slot(g, t, weight_entry(i)), i, i % 2)

            def out_split(v, i):
                base = GROUPS * UNITS * (TPU - 1)
                if i >= 2:
                    act.wait_ge(tile_done, v * (TPU - 1) + base + i - 1)
                elif i == 0:
                    act.wait_ge(tile_done, v * (TPU - 1) + base)
                else:
                    act.wait_ge(acc_done, v * SB + OUT_ACC)
                out_entry_wait(act, v, i)
                hi(i % RING, i, i % 2)

            def take(g, t):
                if t < 2:
                    dst = (q_t, k_t)[t]
                    for j in range(HG):
                        act.wait_ge(acc_done, acc_before(g, t) + j + 1)
                        act.activation(dst[:, j, :], acc[:, j, S:2 * S], ACT.Copy,
                                       scale=(INV_SQRT_D, 1.0)[t]).then_inc(cross_ready, 1)
                elif t == 3:
                    for s in range(SB):
                        act.wait_ge(acc_done, acc_before(g, t) + s + 1)
                        act.activation(z_gate[:, s, :], acc[:, 2 + s, :], ACT.Sigmoid).then_inc(sigma_ready, 1)

            def h_hi(i):
                act.wait_ge(h_ready, i + 1)
                act.activation(act_split[:, i * TK:(i + 1) * TK, 0:S], act_t[:, i * TK:(i + 1) * TK, :], ACT.Copy).then_inc(split_hi, 1)

            def y_hi(i):
                if i == 0:
                    act.wait_ge(acc_done, OUT_ACC)
                act.wait_ge(y_taken, HG * (i + 1))
                act.activation(act_split[:, i * TK:(i + 1) * TK, 0:S], act_t[:, i * TK:(i + 1) * TK, :], ACT.Copy).then_inc(split_hi, 1)

            def probs_job(G, stick, j):
                act.wait_ge(scores_ready, G * HG + j + 1) if stick else None
                if stick:
                    if j >= 2:
                        act.wait_ge(probs_a, G * HG + j - 1)
                    act.activation(keep[:, j % 2, :], att[:, j, 0:KEYS], ACT.Sigmoid, scale=-1.0)
                    act.activation(probs[:, j, :], att[:, j, 0:KEYS], ACT.Sigmoid).then_inc(keep_ready, 1)
                else:
                    act.wait_ge(max_ready, G * HG - SB_HEADS + j + 1)
                    act.activation(probs[:, j, 0:P], probs[:, j, 0:P], ACT.Exp, bias=neg_max[:, j, 0:1])
                    act.activation(probs[:, j, P:KEYS], probs[:, j, P:KEYS], ACT.Exp, bias=neg_max[:, j, 1:2]).then_inc(probs_b, 1)

            def square_job(G, j):
                act.wait_ge(y_ready, G * HG + j + 1)
                for s in range(SB):
                    ins = act.activation(y_nat[:, j, s, :], att[:, j, s * VW:s * VW + P], ACT.Square,
                                         accum_out=sums[:, j, s:s + 1])
                ins.then_inc(y_squared, 1)

            def y_job(G, j):
                act.wait_ge(y_turned, G * HG + j // 2 * 2 + 2)
                act.activation(act_t[:, bass.ds(G * HG + j, 1), :].rearrange("p o s -> p (o s)"),
                               att[:, j // 2, (j % 2) * S:(j % 2 + 1) * S], ACT.Copy,
                               scale=vec_t[:, bass.ds(G * HG + j + 2 * KC, 1)]).then_inc(y_taken, 1)

            def job(G, stick, t, n):
                if t == 0 and n < HG:
                    probs_job(G, stick, n)
                elif t == 2 and n < 2:
                    square_job(G, 2 * n)
                    square_job(G, 2 * n + 1)
                elif t == 3 and n < HG:
                    y_job(G, n)

            def group(g, G, stick):
                for t in range(UNITS):
                    for i in range(TPU):
                        if G is None and t == 0:
                            h_hi(i)
                        split(g, t, i)
                        if i == 0 and not (G is None and t == 0):
                            take(g if t else g - 1, (t - 1) % UNITS)
                        if i >= 1 and G is not None:
                            job(G, stick, t, i - 1)

            group(0, None, None)
            with act.Fori(1, SB_GROUPS + 1) as g:
                group(g, g - 1, True)
            with act.Fori(SB_GROUPS + 1, GROUPS) as g:
                group(g, g - 1, False)

            G = GROUPS - 1
            for i in range(TPU):
                out_split(0, i)
                if i == 0:
                    take(G, 3)
                if i < TPU - 1:
                    y_hi(i)
                if i in (1, 2):
                    probs_job(G, False, 2 * i - 2)
                    probs_job(G, False, 2 * i - 1)
                if i == 4:
                    for j in range(HG):
                        square_job(G, j)
                if i == 6:
                    pass
            for j in range(HG):
                y_job(G, j)
            y_hi(TPU - 1)

            def gate_copy(v, par):
                act.wait_ge(gate_ready, v + 1)
                act.wait_ge(acc_taken, v * SB + OUT_ACC - SB)
                act.activation(gate_row[:, par, :], att[:, 2 + par, :], ACT.Copy).then_inc(gate_copied, 1)

            def square_res(v):
                for s in range(SB):
                    act.wait_ge(res_ready, v * SB + s + 1)
                    act.activation(z_gate[:, s, :], res[:, s, :], ACT.Square,
                                   accum_out=out_sums[:, s, bass.ds(v, 1)]).then_inc(res_squared, 1)

            def out_unit(v, par):
                for i in range(TPU):
                    out_split(v, i)
                    if i == 0:
                        gate_copy(v - 1, 1 - par)
                    if i == 3:
                        square_res(v - 1)

            out_unit(1, 1)
            with act.Fori(1, OUT_UNITS // 2) as i:
                out_unit(i * 2, 0)
                out_unit(i * 2 + 1, 1)
            gate_copy(OUT_UNITS - 1, 1)
            square_res(OUT_UNITS - 1)
            act.wait_ge(out_rstd_ready, 1)
            for n in range(2):
                act.activation(xnew[:, 1, n * D // 2:(n + 1) * D // 2], xnew[:, 1, n * D // 2:(n + 1) * D // 2],
                               ACT.Copy, scale=out_rstd[:, 1:2]).then_inc(scaled_s, 1)

        @block.vector
        def _(dve):
            dve.wait_ge(pos_ready, 3)
            steps = [0]

            def step(ins):
                ins.then_inc(mask_step, 1)
                steps[0] += 1
                dve.wait_ge(mask_step, steps[0])

            low4, low16 = tmp[0].bitcast(I32), tmp[1].bitcast(I32)
            f0, f1 = tmp[2], tmp[3]
            step(dve.tensor_scalar(low4, pos_t, 3, None, ALU.bitwise_and))
            step(dve.tensor_scalar(low16, pos_t, 15, None, ALU.bitwise_and))
            step(dve.tensor_scalar(f0, low4, 0.0, None, ALU.is_equal))
            step(dve.scalar_tensor_tensor(f1, low16, 0.0, f0, ALU.is_equal, ALU.add))
            step(dve.scalar_tensor_tensor(f0, pos_t, float(WINDOW), f1, ALU.is_le, ALU.add))
            step(dve.scalar_tensor_tensor(count_t[:, :], pos_t, 0.0, f0, ALU.is_ge, ALU.mult))
            step(dve.tensor_scalar(causal_t[:, :], pos_t, 0.0, None, ALU.is_gt))
            step(dve.tensor_scalar(stop_mask[:, :], pos_n, 0.0, None, ALU.is_le))
            step(dve.tensor_scalar(low4, pos_n, 3, None, ALU.bitwise_and))
            step(dve.tensor_scalar(f0, low4, 0.0, None, ALU.is_equal))
            step(dve.scalar_tensor_tensor(f1, pos_n, float(WINDOW), f0, ALU.is_le, ALU.max))
            step(dve.scalar_tensor_tensor(f0, pos_n, 0.0, f1, ALU.is_ge, ALU.mult))
            step(dve.tensor_scalar(f1, f0, -MASKED, MASKED, ALU.mult, ALU.add))
            step(dve.tensor_tensor(dist_mask[:, :], f1, pos_n, ALU.subtract))

            assert steps[0] == MASK_STEPS

            dve.wait_ge(vec_turned, 1)
            dve.tensor_copy(vec_t[:, :], att[:, 0, 0:3 * KC]).then_inc(vec_copied, 1)
            dve.wait_ge(c_sigma, 1)
            dve.wait_ge(vec_copied, 1)
            dve.tensor_tensor(c_t[:, :], c_t[:, :], vec_t[:, 0:KC], ALU.mult).then_inc(c_ready, 1)
            dve.wait_ge(c_ready, 1)

            dve.wait_ge(seed_ready, 32)

            def ada(slot, k, sums_of, half):
                cols = sums_of[:, half * (D // 2):(half + 1) * (D // 2)]
                dve.scalar_tensor_tensor(cols, ring[:, slot, :], c_t[:, bass.ds(k, 1)], cols, ALU.mult, ALU.add).then_inc(ring_used, 1)

            for n in range(RING):
                dve.wait_ge(raw_ready[n], 16)
                if n >= 2:
                    dve.wait_ge(ring_used, n - 1)
                ada(n, n // 2, ada_acc, n % 2)
            with dve.Fori(1, KC // 2) as i:
                for n in range(RING):
                    dve.wait_ge(raw_ready[n], i * 16 + 16)
                    dve.wait_ge(ring_used, i * RING + n - 1)
                    ada(n, i * 2 + n // 2, ada_acc, n % 2)
            with dve.Fori(0, KC // 2) as i:
                for n in range(RING):
                    dve.wait_ge(raw_ready[n], i * 16 + 16 * (KC // 2 + 1))
                    dve.wait_ge(ring_used, i * RING + 2 * KC + n - 1)
                    ada(n, i * 2 + n // 2, shift_acc, n % 2)
            dve.wait_ge(mod_summed, 1)
            dve.scalar_tensor_tensor(mul_t[:, :], att[:, 1, 0:KC], 1.0, vec_t[:, KC:2 * KC], ALU.add, ALU.mult).then_inc(mod_ready, 1)
            for b in range(2):
                dve.wait_ge(mod_summed, 2 + b)
                dve.tensor_copy(add_t[:, b * KC // 2:(b + 1) * KC // 2], att[:, 2 + b, 0:KC // 2]).then_inc(mod_ready, 1)
                if b == 0:
                    dve.wait_ge(x_copied, 2 * TPU)
            dve.wait_ge(mod_ready, 3)

            def h_chunks(i):
                for k in range(i * TK, (i + 1) * TK):
                    ins = dve.tensor_scalar(act_t[:, k, :], act_t[:, k, :], mul_t[:, k:k + 1], add_t[:, k:k + 1], ALU.mult, ALU.add)
                ins.then_inc(h_ready, 1)

            def act_lo(i, n):
                dve.wait_ge(split_hi, n + 1)
                if n < TPU:
                    dve.wait_ge(h_ready, n + 1)
                dve.tensor_tensor(act_split[:, i * TK:(i + 1) * TK, S:2 * S], act_t[:, i * TK:(i + 1) * TK, :],
                                  act_split[:, i * TK:(i + 1) * TK, 0:S].bitcast(F32), ALU.subtract).then_inc(split_lo, 1)

            def lo(slot, par):
                dve.tensor_tensor(w_lo[:, par, :, :].rearrange("p k e -> p (k e)"), ring[:, slot, :],
                                  w_hi[:, par, :, :].rearrange("p k e -> p (k e)").bitcast(F32), ALU.subtract).then_inc(ring_used, 1)

            def split(g, t, i):
                dve.wait_ge(hi_ready, g * (UNITS * TPU) + t * TPU + i + 1)
                lo(entry_slot(g, t, weight_entry(i)), i % 2)

            def out_split(v, i):
                dve.wait_ge(hi_ready, v * TPU + GROUPS * UNITS * TPU + i + 1)
                lo(i % RING, i % 2)

            def gate(g, t, half):
                e = (TPU // 2, ENTRIES - 1)[half]
                entry_wait(dve, g, t, e)
                cols = ada_acc[:, half * (D // 2):(half + 1) * (D // 2)]
                dve.scalar_tensor_tensor(cols, ring[:, entry_slot(g, t, e), :], c_t[:, bass.ds(g * UNITS + t, 1)], cols,
                                         ALU.mult, ALU.add).then_inc(ring_used, 1)

            def take(g, t):
                if t < 2:
                    dst = (q_t, k_t)[t]
                    for j in range(HG):
                        dve.wait_ge(cross_ready, g * (2 * HG) + t * HG + j + 1)
                        if t == 0:
                            dve.scalar_tensor_tensor(dst[:, j, :], acc[:, j, 0:S], INV_SQRT_D, dst[:, j, :],
                                                     ALU.mult, ALU.add).then_inc(acc_taken, 1)
                        else:
                            dve.tensor_tensor(dst[:, j, :], acc[:, j, 0:S], dst[:, j, :], ALU.add).then_inc(acc_taken, 1)
                elif t == 2:
                    for s in range(SB):
                        dve.wait_ge(acc_done, acc_before(g, t) + s + 1)
                        dve.tensor_copy(v_ones[:, s, :, 0:P], acc[:, s, :].rearrange("p (j e) -> p j e", j=HG)).then_inc(acc_taken, 1)
                else:
                    for s in range(SB):
                        dve.wait_ge(sigma_ready, g * SB + s + 1)
                        dve.tensor_tensor(z_gate[:, s, :], acc[:, 2 + s, :], z_gate[:, s, :], ALU.mult).then_inc(acc_taken, 1)

            def probs_job(G, stick, j):
                if stick:
                    dve.wait_ge(keep_ready, G * HG + j + 1)
                    dve.tensor_tensor_scan(left[:, j % 2, 0:P][:, ::-1], keep[:, j % 2, 0:P][:, ::-1],
                                           stop_mask[:, 0:P][:, ::-1], 1.0, ALU.mult, ALU.max)
                    dve.tensor_tensor_scan(left[:, j % 2, P + 1:KEYS + 1][:, ::-1], keep[:, j % 2, P:KEYS][:, ::-1],
                                           stop_mask[:, P:KEYS][:, ::-1], 1.0, ALU.mult, ALU.max).then_inc(left_ready, 1)
                    dve.wait_ge(left_ready, G * HG + j + 1)
                    dve.tensor_tensor(probs[:, j, 0:P], probs[:, j, 0:P], left[:, j % 2, 1:P + 1], ALU.mult)
                    dve.tensor_tensor(probs[:, j, P:KEYS], probs[:, j, P:KEYS], left[:, j % 2, P + 2:KEYS + 2],
                                      ALU.mult).then_inc(probs_a, 1)
                else:
                    n = G * HG - SB_HEADS + j
                    dve.wait_ge(scores_ready, G * HG + j + 1)
                    dve.scalar_tensor_tensor(probs[:, j, :], dist_mask[:, :], slope[:, bass.ds(n, 1)], att[:, j, 0:KEYS],
                                             ALU.mult, ALU.add).then_inc(biased, 1)
                    dve.wait_ge(biased, n + 1)
                    dve.tensor_reduce(neg_max[:, j, 0:1], probs[:, j, 0:P], AX.X, ALU.max, negate=True)
                    dve.tensor_reduce(neg_max[:, j, 1:2], probs[:, j, P:KEYS], AX.X, ALU.max, negate=True).then_inc(max_ready, 1)

            def turned_job(G, stick, j):
                dve.wait_ge(probs_turned, G * HG + j + 1)
                dve.tensor_tensor(probs_t[:, j, :], att[:, j, 0:KEYS], (causal_t if stick else count_t)[:, :],
                                  ALU.mult).then_inc(probs_t_ready, 1)

            def variance_job(G, stick):
                dve.wait_ge(y_squared, G * HG + HG)
                if stick:
                    dve.tensor_scalar(sums[:, :, :], sums[:, :, :], 1.0 / P, EPS, ALU.mult, ALU.add).then_inc(var_ready, 1)
                    return
                n = G * 2 - 2 * SB_GROUPS
                for s in range(SB):
                    ins = dve.tensor_copy(dens[:, :, s:s + 1], att[:, :, s * VW + P:s * VW + P + 1])
                ins.then_inc(den_step, 1)
                dve.wait_ge(den_step, n + 1)
                dve.scalar_tensor_tensor(den_sq[:, :, :], dens[:, :, :], EPS, dens[:, :, :], ALU.mult, ALU.mult).then_inc(den_step, 1)
                dve.wait_ge(den_step, n + 2)
                dve.scalar_tensor_tensor(sums[:, :, :], sums[:, :, :], 1.0 / P, den_sq[:, :, :], ALU.mult, ALU.add).then_inc(var_ready, 1)

            def norm_job(G, j):
                if j == 0:
                    dve.wait_ge(rstd_ready, G + 1)
                for s in range(SB):
                    ins = dve.scalar_tensor_tensor(y_nat[:, j, s, :], att[:, j, s * VW:s * VW + P], rstd[:, j, s:s + 1],
                                                   z_gate[:, s, j * P:(j + 1) * P], ALU.mult, ALU.mult)
                ins.then_inc(y_normed, 1)

            def job(G, stick, t, n):
                if t == 0 and n < HG:
                    probs_job(G, stick, n)
                elif t == 1 and n < HG:
                    turned_job(G, stick, n)
                elif t == 2 and n == 2:
                    variance_job(G, stick)
                elif t == 2 and n in (3, 4):
                    norm_job(G, 2 * n - 6)
                    norm_job(G, 2 * n - 5)

            def group(g, G, stick):
                for t in range(UNITS):
                    for i in range(TPU):
                        if G is None and t == 0:
                            h_chunks(i)
                        split(g, t, i)
                        if G is None and t == 0:
                            act_lo(i, i)
                        elif i == 0:
                            take(g if t else g - 1, (t - 1) % UNITS)
                        if i >= 1 and G is not None:
                            job(G, stick, t, i - 1)
                        if i == TPU // 2 - 1:
                            if G is None and t == 0:
                                dve.wait_ge(gate_seeded, 16)
                            gate(g, t, 0)
                        if i == TPU - 1:
                            gate(g, t, 1)

            group(0, None, None)
            dve.wait_ge(ones_set, 1)
            with dve.Fori(1, SB_GROUPS + 1) as g:
                group(g, g - 1, True)
            with dve.Fori(SB_GROUPS + 1, GROUPS) as g:
                group(g, g - 1, False)

            G = GROUPS - 1
            for i in range(TPU):
                out_split(0, i)
                if i == 0:
                    take(G, 3)
                if i < TPU - 1:
                    act_lo(i, TPU + i)
                if i in (1, 2):
                    probs_job(G, False, 2 * i - 2)
                    probs_job(G, False, 2 * i - 1)
                if i == 3:
                    for j in range(HG):
                        turned_job(G, False, j)
                if i == 4:
                    variance_job(G, False)
                if i == 5:
                    for j in range(HG):
                        norm_job(G, j)
            act_lo(TPU - 1, 2 * TPU - 1)

            def finish(v, par):
                dve.wait_ge(gate_copied, v + 1)
                dve.wait_ge(xg_ready, v * 32 + 32)
                if not isinstance(v, int) or v:
                    dve.wait_ge(res_squared, v * SB)
                    dve.wait_ge(gained, v * SB)
                cols = bass.ds(v * GW, GW)
                for s in range(SB):
                    dve.wait_ge(acc_done, v * SB + OUT_ACC + s + 1)
                    dve.tensor_tensor(res[:, s, :], acc[:, 2 * par + s, :], gate_row[:, par, :], ALU.mult).then_inc(acc_taken, 1)
                for s in range(SB):
                    dve.wait_ge(acc_taken, v * SB + OUT_ACC + s + 1)
                    dve.tensor_tensor(res[:, s, :], res[:, s, :], xnew[:, s, cols], ALU.add).then_inc(res_ready, 1)
                for s in range(SB):
                    dve.wait_ge(res_ready, v * SB + s + 1)
                    dve.tensor_tensor(xnew[:, s, cols], res[:, s, :], g_final_row[:, :], ALU.mult).then_inc(gained, 1)

            def out_unit(v, par):
                for i in range(TPU):
                    out_split(v, i)
                    if i == 1:
                        finish(v - 1, 1 - par)

            out_unit(1, 1)
            with dve.Fori(1, OUT_UNITS // 2) as i:
                out_unit(i * 2, 0)
                out_unit(i * 2 + 1, 1)
            finish(OUT_UNITS - 1, 1)
            dve.wait_ge(res_squared, OUT_UNITS * SB)
            dve.reduce_sum(out_sum[:, :], out_sums[:, :, :], AX.X).then_inc(tail_step, 1)
            dve.wait_ge(tail_step, 1)
            dve.tensor_scalar(out_sum[:, :], out_sum[:, :], 1.0 / D, EPS, ALU.mult, ALU.add).then_inc(tail_step, 1)
            dve.wait_ge(out_rstd_ready, 1)
            dve.wait_ge(gained, OUT_UNITS * SB)
            for n in range(2):
                dve.tensor_scalar(xnew[:, 0, n * D // 2:(n + 1) * D // 2], xnew[:, 0, n * D // 2:(n + 1) * D // 2],
                                  out_rstd[:, 0:1], None, ALU.mult).then_inc(scaled_v, 1)

        @block.tensor
        def _(pe):
            pe.wait_ge(ident_ready, 3)
            pe.wait_ge(vec_ready, 64)
            pe.transpose(att[:, 0, 0:3 * KC], vec_rows[:, :], ident[0:3 * KC, 0:3 * KC]).then_inc(vec_turned, 1)
            for s in range(SB):
                pe.wait_ge(x_stat, 3 * (s + 1))
                for b in range(TPU):
                    n = s * TPU + b
                    if n >= 4:
                        pe.wait_ge(x_copied, n - 3)
                    for k in range(TK):
                        kc = b * TK + k
                        mm = pe.matmul(acc[:, b % 4, k * P:(k + 1) * P], x_half[:, kc * P:(kc + 1) * P], diag[:, :],
                                       start=True, stop=True)
                    mm.then_inc(x_turned, 1)
            pe.wait_ge(ring_used, 2 * KC)
            for k in range(KC):
                mm = pe.matmul(att[:, 1, k:k + 1], ada_acc[:, k * P:(k + 1) * P], ones[:, 0:1], start=True, stop=True)
            mm.then_inc(mod_summed, 1)
            for b in range(2):
                pe.wait_ge(ring_used, 4 * KC - 1 + b)
                for k in range(KC // 2):
                    kc = b * KC // 2 + k
                    mm = pe.matmul(att[:, 2 + b, k:k + 1], shift_acc[:, kc * P:(kc + 1) * P], ones[:, 0:1], start=True, stop=True)
                mm.then_inc(mod_summed, 1)

            def turned_tile(i, w, last):
                for kk in range(TK):
                    k = i * TK + kk
                    for e in range(HG):
                        pe.matmul(acc[:, e, :], w_hi[:, w, kk, e * P:(e + 1) * P], act_split[:, k, :],
                                  start=(k == 0), stop=False, skip_group_check=True)
                        mm = pe.matmul(acc[:, e, 0:S], w_lo[:, w, kk, e * P:(e + 1) * P], act_split[:, k, 0:S],
                                       start=False, stop=(k == KC - 1), skip_group_check=True)
                        if last and kk == TK - 1:
                            mm.then_inc(acc_done, 1)
                if not last:
                    mm.then_inc(tile_done, 1)

            def rows_tile(i, w, last, bank):
                for kk in range(TK):
                    k = i * TK + kk
                    for s in range(SB):
                        a_hi = act_split[:, k, s * P:(s + 1) * P]
                        a_lo = act_split[:, k, S + s * P:S + (s + 1) * P]
                        pe.matmul(acc[:, bank + s, :], a_hi, w_hi[:, w, kk, :], start=(k == 0), stop=False)
                        pe.matmul(acc[:, bank + s, :], a_hi, w_lo[:, w, kk, :], start=False, stop=False)
                        mm = pe.matmul(acc[:, bank + s, :], a_lo, w_hi[:, w, kk, :], start=False, stop=(k == KC - 1))
                        if last and kk == TK - 1:
                            mm.then_inc(acc_done, 1)
                if not last:
                    mm.then_inc(tile_done, 1)

            def unit(g, t, first):
                if t == 0 and not first:
                    pe.wait_ge(acc_taken, g * ACC_PER_GROUP)
                elif t == 1:
                    pe.wait_ge(acc_taken, g * ACC_PER_GROUP + ACC_AT[1])
                elif t == 2:
                    pe.wait_ge(acc_taken, g * ACC_PER_GROUP + ACC_AT[1] + SB)
                elif t == 3:
                    pe.wait_ge(acc_taken, g * ACC_PER_GROUP + ACC_AT[2])
                for i in range(TPU):
                    pe.wait_ge(ring_used, g * (UNITS * ENTRIES) + PROJ_BASE + t * ENTRIES + weight_entry(i) + 1)
                    if first and t == 0:
                        pe.wait_ge(split_lo, i + 1)
                    if t < 2:
                        turned_tile(i, i % 2, i == TPU - 1)
                    else:
                        rows_tile(i, i % 2, i == TPU - 1, 2 * (t - 2))

            def scores(g, first):
                pe.wait_ge(acc_taken, g * ACC_PER_GROUP + ACC_AT[2])
                if not first:
                    pe.wait_ge(y_taken, g * HG)
                for j in range(HG):
                    pe.matmul(att[:, j, 0:P], q_t[:, j, 0:P], k_t[:, j, 0:P], start=True, stop=True)
                    pe.matmul(att[:, j, P:KEYS], q_t[:, j, P:S], k_t[:, j, :], start=True, stop=True).then_inc(scores_ready, 1)

            def turn_probs(G, stick):
                for j in range(HG):
                    if stick:
                        pe.wait_ge(probs_a, G * HG + j + 1)
                    else:
                        pe.wait_ge(probs_b, G * HG - SB_HEADS + j + 1)
                    for b in range(3):
                        mm = pe.transpose(att[:, j, b * P:(b + 1) * P], probs[:, j, b * P:(b + 1) * P], ident[:, :])
                    mm.then_inc(probs_turned, 1)

            def values(G):
                pe.wait_ge(acc_taken, G * ACC_PER_GROUP + ACC_AT[3])
                for j in range(HG):
                    pe.wait_ge(probs_t_ready, G * HG + j + 1)
                    pe.matmul(att[:, j, 0:VW], probs_t[:, j, 0:P], v_ones[:, 0, j, :], start=True, stop=True)
                    pe.matmul(att[:, j, VW:2 * VW], probs_t[:, j, P:2 * P], v_ones[:, 0, j, :], start=True, stop=False)
                    pe.matmul(att[:, j, VW:2 * VW], probs_t[:, j, 2 * P:KEYS], v_ones[:, 1, j, :], start=False, stop=True).then_inc(y_ready, 1)

            def turn_y(G):
                pe.wait_ge(y_normed, G * HG + HG)
                for j in range(HG):
                    for s in range(SB):
                        mm = pe.transpose(att[:, j // 2, (j % 2) * S + s * P:(j % 2) * S + (s + 1) * P], y_nat[:, j, s, :], ident[:, :])
                    mm.then_inc(y_turned, 1)

            def group(g, G, stick):
                for t in range(UNITS):
                    unit(g, t, G is None)
                    if t == 0 and G is not None:
                        turn_probs(G, stick)
                    if t == 1 and G is not None:
                        values(G)
                    if t == 2 and G is not None:
                        turn_y(G)
                    if t == 3:
                        scores(g, G is None)

            group(0, None, None)
            pe.wait_ge(ones_set, 1)
            with pe.Fori(1, SB_GROUPS + 1) as g:
                group(g, g - 1, True)
            with pe.Fori(SB_GROUPS + 1, GROUPS) as g:
                group(g, g - 1, False)

            G = GROUPS - 1

            def out_unit(v, par, first=False):
                pe.wait_ge(acc_taken, v * SB + OUT_ACC - SB)
                for i in range(TPU):
                    if first and i == 4:
                        turn_probs(G, False)
                    if first and i == 5:
                        values(G)
                    if i == TPU - 1:
                        if first:
                            turn_y(G)
                        else:
                            pe.wait_ge(gate_copied, v - 1) if not isinstance(v, int) or v > 1 else None
                        pe.matmul(att[:, 2 + par, :], ones[:, :], ada_acc[:, bass.ds(v * GW, GW)], start=True, stop=True).then_inc(gate_ready, 1)
                    pe.wait_ge(ring_used, v * TPU + OUT_BASE + i + 1)
                    if first:
                        pe.wait_ge(split_lo, TPU + i + 1)
                    rows_tile(i, i % 2, i == TPU - 1, 2 * par)

            out_unit(0, 0, first=True)
            out_unit(1, 1)
            with pe.Fori(1, OUT_UNITS // 2) as i:
                out_unit(i * 2, 0)
                out_unit(i * 2 + 1, 1)


_INS = ["x", "c", "w_ada", "b_ada", "g_norm", "w_in", "g_sb", "g_dil", "w_out", "g_final"]


def kernel(**inputs):
    import concourse.bacc as bacc
    from concourse.bass_utils import run_bass_kernel_spmd

    nc = bacc.Bacc("TRN2", target_bir_lowering=False, num_devices=1, dynamic_dma_scratch_size=1024)
    arrays, args = {}, []
    for name in _INS:
        a = np.ascontiguousarray(inputs[name])
        arrays[f"in_{name}"] = a
        args.append(nc.dram_tensor(f"in_{name}", a.shape, mybir.dt.from_np(a.dtype), kind="ExternalInput").ap())
    shape = inputs["x"].shape
    args.append(nc.dram_tensor("out", shape, F32, kind="ExternalOutput").ap())
    build(nc, *args)
    r = run_bass_kernel_spmd(nc, [arrays], core_ids=[0])
    return r.results[0]["out"]
```

```python
from contextlib import ExitStack

import numpy as np
import concourse.bass as bass
from concourse import mybir

F32 = mybir.dt.float32
F32R = mybir.dt.float32r
BF16 = mybir.dt.bfloat16
I32 = mybir.dt.int32
ALU = mybir.AluOpType
ACT = mybir.ActivationFunctionType
AX = mybir.AxisListType

P = 128
S = 256
SB = S // P
D = 4096
KC = D // P
HEADS = 32
SB_HEADS = 16
HG = 4
GW = HG * P
GROUPS = HEADS // HG
SB_GROUPS = SB_HEADS // HG
PARTS = 4
UNITS = 3
TK = 4
TPU = KC // TK
TILE = TK * GW
RING = 4
PHASES = D // GW
ADA_TILES = 2 * TPU
ORDER = [("q", 0)] + [("z", G) for G in range(GROUPS)] + [("k", 0), ("v", 0)]
Z0, NZ = 1, GROUPS
PHASE = "a" * (ADA_TILES - len(ORDER) + 1) + "w" + "aw" * (len(ORDER) - 1)
LAST = "wwwwgwwgwwgwwgw"
assert PHASE.count("a") == ADA_TILES and PHASE.count("w") == LAST.count("w") == len(ORDER)
assert len(PHASE) % RING == len(LAST) % RING == RING - 1
FIRST_ENTRIES = ADA_TILES
PHASE_USES = len(PHASE)
LAST_BASE = FIRST_ENTRIES + (PHASES - 1) * (PHASE_USES + 1)
LAST_USES = FIRST_ENTRIES + (PHASES - 1) * PHASE_USES
SKIPPED = PHASES
WIDE = [[2, 5, 8, 11], [2, 5, 8, 11], [2, 5, 8, 11]]
NARROW = [[3, 8], [4], [4]]
WIDE_GROUPS = SB_GROUPS + 1
OUT_UNITS = D // GW
WIDE_GATES = sum(len(u) for u in WIDE)
NARROW_GATES = sum(len(u) for u in NARROW)
WIDE_ENTRIES = UNITS * TPU + WIDE_GATES
NARROW_ENTRIES = UNITS * TPU + NARROW_GATES
PROJ_BASE = LAST_BASE + len(LAST) + 1
NARROW_BASE = PROJ_BASE + (WIDE_GROUPS - 1) * WIDE_ENTRIES
OUT_BASE = NARROW_BASE + (GROUPS - WIDE_GROUPS) * NARROW_ENTRIES
assert all(n % RING == 0 for n in (FIRST_ENTRIES, LAST_BASE, WIDE_ENTRIES, NARROW_ENTRIES, PROJ_BASE))
GATE_LAST = LAST.count("g") // 2
GATE_WIDE = WIDE_GATES // 2
GATE_NARROW = NARROW_GATES // 2
GATE_BASE_NARROW = GATE_LAST + (WIDE_GROUPS - 1) * GATE_WIDE
assert GATE_BASE_NARROW + (GROUPS - WIDE_GROUPS) * GATE_NARROW == KC
KEYS = 3 * P
VW = P + 1
EPS = 1e-6
INV_SQRT_D = float(P) ** -0.5
SLOPES = [2.0 ** (-8.0 * (h + 1) / (HEADS - SB_HEADS)) for h in range(HEADS - SB_HEADS)]
MASKED = -1.0e30
WINDOW = 128
ACC_PER_GROUP = 2 * HG + SB
ACC_AT = [0, HG, 2 * HG]
ACC_FIRST = 2 * 3
OUT_ACC = ACC_FIRST + (GROUPS - 1) * ACC_PER_GROUP
TILES_FIRST = 3 * (TPU - 1)
W_FIRST = TPU * len(ORDER)
OUT_TILES = TILES_FIRST + (GROUPS - 1) * UNITS * (TPU - 1)
STORES = [(0, D // 4), (D // 4, D // 2), (D // 2, D)]
MASK_STEPS = 14


def build(nc, x, c, w_ada, b_ada, g_norm, w_in, g_sb, g_dil, w_out, g_final, out):
    x_rows = x.rearrange("o (s p) d -> p (o s) d", p=P)
    out_rows = out.rearrange("o (s p) d -> p (o s) d", p=P)
    ada_rows = w_ada.rearrange("l (k p) e -> (l k) p e", p=P)
    ada_tiles = w_ada.rearrange("l (t k p) e -> (l t) p k e", p=P, k=TK)
    in_tiles = w_in.rearrange("l (t k p) e -> (l t) p k e", p=P, k=TK)
    out_tiles = w_out.rearrange("l (t k p) e -> (l t) p k e", p=P, k=TK)

    with ExitStack() as ctx:
        def sb(name, shape, dt=F32):
            return ctx.enter_context(nc.sbuf_tensor(name, shape, dt))

        def sem(name):
            return ctx.enter_context(nc.semaphore(name))

        act_split = sb("act_split", [P, KC, 2 * S], F32R)
        act_t = sb("act_t", [P, KC, S])
        xnew = act_t[:, :, :].rearrange("p k s -> p (k s)").rearrange("p (s d) -> p s d", s=SB)
        ring = sb("ring", [P, RING, TILE])
        w_hi = sb("w_hi", [P, 2, TK, GW], F32R)
        w_lo = sb("w_lo", [P, 2, TK, GW], F32R)
        ada_acc = sb("ada_acc", [P, D])
        mod_acc = ada_acc[:, :].rearrange("p (j kk a e) -> p j kk a e", j=2, kk=2, a=2)
        heads_in = sb("heads_in", [P, 4, HG * S])
        q_t = heads_in[:, 0, :].rearrange("p (j s) -> p j s", j=HG)
        k_t = heads_in[:, 1, :].rearrange("p (j s) -> p j s", j=HG)
        squares = heads_in[:, 2, :].rearrange("p (s e) -> p s e", s=SB)
        y_nat = heads_in[:, 3, :].rearrange("p (j s d) -> p j s d", j=HG, s=SB)
        gate_row = heads_in[:, 0, :].rearrange("p (a e) -> p a e", a=2)
        res = heads_in[:, 1, :].rearrange("p (s e) -> p s e", s=SB)
        v_ones = sb("v_ones", [P, SB, HG, VW])
        attn = sb("attn", [P, 2 * HG * KEYS + 2 * KEYS + 2 * (KEYS + 2)])
        probs = attn[:, 0:HG * KEYS].rearrange("p (j c) -> p j c", j=HG)
        probs_t = attn[:, HG * KEYS:2 * HG * KEYS].rearrange("p (j c) -> p j c", j=HG)
        at = 2 * HG * KEYS
        keep = attn[:, at:at + 2 * KEYS].rearrange("p (a c) -> p a c", a=2)
        at += 2 * KEYS
        left = attn[:, at:at + 2 * (KEYS + 2)].rearrange("p (a c) -> p a c", a=2)
        z_sums = [heads_in[:, n, :] for n in (0, 1, 3)] + [
            attn[:, n * HG * S:(n + 1) * HG * S] for n in range(4)] + [heads_in[:, 2, :]]
        z_part = v_ones
        x_half = attn[:, 0:D]
        scratch = act_t[:, :, :].rearrange("p k s -> p (k s)")
        pos_t = scratch[:, 0:KEYS].bitcast(I32)
        pos_n = scratch[:, KEYS:2 * KEYS].bitcast(I32)
        tmp = [scratch[:, (2 + i) * KEYS:(3 + i) * KEYS] for i in range(4)]
        g_final_row = sb("g_final_row", [P, GW])
        ident = sb("ident", [P, P])
        diag = sb("diag", [P, P])
        ones = sb("ones", [P, P])
        stop_mask = sb("stop_mask", [P, KEYS], BF16)
        dist_mask = sb("dist_mask", [P, KEYS], BF16)
        causal_t = sb("causal_t", [P, KEYS], BF16)
        count_t = sb("count_t", [P, KEYS], BF16)
        vec_rows = sb("vec_rows", [3 * KC, P])
        vec_t = sb("vec_t", [P, 3 * KC])
        bias_rows = sb("bias_rows", [2 * KC, P])
        bias_t = sb("bias_t", [P, PHASES, 2, TK])
        c_t = sb("c_t", [P, KC])
        mod_t = sb("mod_t", [P, 2, TK])
        mul_t = sb("mul_t", [P, TK])
        slope = sb("slope", [P, len(SLOPES)])
        neg_max = sb("neg_max", [P, HG, SB])
        sums = sb("sums", [P, HG, SB])
        dens = sb("dens", [P, HG, SB])
        den_sq = sb("den_sq", [P, HG, SB])
        rstd = sb("rstd", [P, HG, SB])
        minus_half = sb("minus_half", [P, HG, SB])
        x_sum = sb("x_sum", [P, SB])
        out_sums = sb("out_sums", [P, SB, OUT_UNITS])
        out_sum = sb("out_sum", [P, SB])
        out_rstd = sb("out_rstd", [P, SB])

        acc = ctx.enter_context(nc.psum_tensor("acc", [P, 4, 512], F32))
        att = ctx.enter_context(nc.psum_tensor("att", [P, 4, 512], F32))

        raw_ready = [sem(f"raw_ready{i}") for i in range(RING)]
        ring_used = sem("ring_used")
        hi_ready = sem("hi_ready")
        tile_done = sem("tile_done")
        z_part_done = sem("z_part_done")
        z_part_taken = sem("z_part_taken")
        z_summed = sem("z_summed")
        sigma_ready = sem("sigma_ready")
        z_ready = sem("z_ready")
        acc_done = sem("acc_done")
        cross_ready = sem("cross_ready")
        acc_taken = sem("acc_taken")
        vec_ready = sem("vec_ready")
        gate_seeded = sem("gate_seeded")
        x_ready = sem("x_ready")
        ident_ready = sem("ident_ready")
        zeroed = sem("zeroed")
        pos_ready = sem("pos_ready")
        mask_step = sem("mask_step")
        vec_turned = sem("vec_turned")
        vec_copied = sem("vec_copied")
        c_sigma = sem("c_sigma")
        c_ready = sem("c_ready")
        x_squared = sem("x_squared")
        x_stat = sem("x_stat")
        x_turned = sem("x_turned")
        x_copied = sem("x_copied")
        mod_part = sem("mod_part")
        mod_summed = sem("mod_summed")
        mod_ready = sem("mod_ready")
        h_ready = sem("h_ready")
        split_hi = sem("split_hi")
        split_lo = sem("split_lo")
        ones_set = sem("ones_set")
        scores_ready = sem("scores_ready")
        keep_ready = sem("keep_ready")
        left_ready = sem("left_ready")
        probs_a = sem("probs_a")
        biased = sem("biased")
        max_ready = sem("max_ready")
        probs_b = sem("probs_b")
        probs_turned = sem("probs_turned")
        probs_t_ready = sem("probs_t_ready")
        y_ready = sem("y_ready")
        y_squared = sem("y_squared")
        den_step = sem("den_step")
        var_ready = sem("var_ready")
        rstd_ready = sem("rstd_ready")
        y_normed = sem("y_normed")
        y_turned = sem("y_turned")
        y_taken = sem("y_taken")
        gate_ready = sem("gate_ready")
        gate_copied = sem("gate_copied")
        xg_ready = sem("xg_ready")
        res_ready = sem("res_ready")
        gained = sem("gained")
        res_squared = sem("res_squared")
        tail_step = sem("tail_step")
        out_rstd_ready = sem("out_rstd_ready")
        scaled_v = sem("scaled_v")
        scaled_s = sem("scaled_s")
        out_done = sem("out_done")

        def acc_before(g, t):
            return g * ACC_PER_GROUP + ACC_AT[t] + ACC_FIRST - ACC_PER_GROUP

        def gates_at(wide, t):
            return (WIDE if wide else NARROW)[t]

        def unit_entry(wide, t):
            return sum(TPU + len(gates_at(wide, u)) for u in range(t))

        def weight_entry(wide, t, i):
            return unit_entry(wide, t) + [e for e in range(2 * TPU) if e not in gates_at(wide, t)][i]

        def group_uses(g, wide):
            if wide:
                return g * WIDE_ENTRIES + PROJ_BASE - SKIPPED - WIDE_ENTRIES
            return g * NARROW_ENTRIES + NARROW_BASE - SKIPPED - WIDE_GROUPS * NARROW_ENTRIES

        def freed(e):
            return e - RING + 1 + (e < RING - 1)

        def landed(n, skipped=SKIPPED):
            return 16 * (n // RING + 1 - (skipped if n % RING == RING - 1 else 0))

        def phase_wait(eng, j, e):
            per = (PHASE_USES + 1) // RING - (e % RING == RING - 1)
            eng.wait_ge(raw_ready[e % RING], j * (16 * per) + landed(FIRST_ENTRIES + e, 0) - 16 * per)

        def last_wait(eng, e):
            eng.wait_ge(raw_ready[e % RING], landed(LAST_BASE + e, PHASES - 1))

        def entry_wait(eng, g, wide, n):
            per, base = (WIDE_ENTRIES, PROJ_BASE - WIDE_ENTRIES) if wide else (
                NARROW_ENTRIES, NARROW_BASE - WIDE_GROUPS * NARROW_ENTRIES)
            eng.wait_ge(raw_ready[n % RING], g * (16 * per // RING) + landed(base + n))

        def out_entry_wait(eng, v, e):
            eng.wait_ge(raw_ready[e % RING], v * (16 * TPU // RING) + landed(OUT_BASE + e))

        def positions(kind, entries):
            return [e for e, k in enumerate(entries) if k == kind]

        def z_set(u):
            return act_t[:, u * TK:(u + 1) * TK, :].rearrange("p k s -> p (k s)")

        block = ctx.enter_context(nc.Block())

        @block.sync
        def _(sp):
            def tile(slot, src):
                sp.dma_start(ring[:, slot, :].rearrange("p (k e) -> p k e", k=TK), src).then_inc(raw_ready[slot], 16)

            def gate(slot, k, half):
                lo = 2 * D + half * (D // 2)
                sp.dma_start(ring[:, slot, :], ada_rows[k, :, lo:lo + D // 2]).then_inc(raw_ready[slot], 16)

            def in_col(g_part, g_rest, t):
                return g_part * (PARTS * SB_HEADS * P) + g_rest * GW + t * SB_HEADS * P

            for n in range(ADA_TILES):
                if n >= RING:
                    sp.wait_ge(ring_used, n - RING + 1)
                tile(n % RING, ada_tiles[n // 2, :, :, n % 2 * D:n % 2 * D + GW])
            def order_col(r):
                name, G = ORDER[r]
                return in_col(G // SB_GROUPS, G % SB_GROUPS, "qkvz".index(name))

            with sp.Fori(1, PHASES) as j:
                for e, kind in enumerate(PHASE):
                    sp.wait_ge(ring_used, j * PHASE_USES + FIRST_ENTRIES - PHASE_USES + freed(e))
                    if kind == "a":
                        n = positions("a", PHASE).index(e)
                        tile(e % RING, ada_tiles[n // 2, :, :, bass.ds(j * GW + n % 2 * D, GW)])
                    else:
                        col = order_col(positions("w", PHASE).index(e))
                        tile(e % RING, in_tiles[j - 1, :, :, col:col + GW])
            for e, kind in enumerate(LAST):
                sp.wait_ge(ring_used, LAST_USES + freed(e))
                if kind == "w":
                    col = order_col(positions("w", LAST).index(e))
                    tile(e % RING, in_tiles[TPU - 1, :, :, col:col + GW])
                else:
                    n = positions("g", LAST).index(e)
                    gate(e % RING, n // 2, n % 2)

            def group(g, wide, part, rest):
                ng = 0
                for t in range(UNITS):
                    i = 0
                    for e in range(TPU + len(gates_at(wide, t))):
                        n = unit_entry(wide, t) + e
                        sp.wait_ge(ring_used, group_uses(g, wide) + freed(n))
                        if e in gates_at(wide, t):
                            first = (GATE_WIDE, GATE_LAST - GATE_WIDE) if wide else (
                                GATE_NARROW, GATE_BASE_NARROW - WIDE_GROUPS * GATE_NARROW)
                            gate(n % RING, g * first[0] + first[1] + ng // 2, ng % 2)
                            ng += 1
                        else:
                            tile(n % RING, in_tiles[i, :, :, bass.ds(in_col(part, rest, t), GW)])
                            i += 1

            with sp.Fori(1, SB_GROUPS) as g:
                group(g, True, 0, g)
            group(SB_GROUPS, True, 1, 0)
            with sp.Fori(WIDE_GROUPS, GROUPS) as g:
                group(g, False, 1, g - SB_GROUPS)

            def out_piece(v):
                sp.dma_start(g_final_row[:, :], g_final[bass.ds(v * GW, GW)].rearrange("(o e) -> o e", o=1)
                             .to_broadcast([P, GW])).then_inc(xg_ready, 16)
                sp.wait_ge(split_lo, 2 * TPU)
                sp.dma_start(xnew[:, :, bass.ds(v * GW, GW)], x_rows[:, :, bass.ds(v * GW, GW)]).then_inc(xg_ready, 16)

            def out_unit(v, first=False):
                for e in range(TPU):
                    sp.wait_ge(ring_used, v * TPU + OUT_BASE - SKIPPED + e - RING + 1)
                    sp.dma_start(ring[:, e % RING, :].rearrange("p (k e) -> p k e", k=TK),
                                 out_tiles[e, :, :, bass.ds(v * GW, GW)]).then_inc(raw_ready[e % RING], 16)
                    if e == 0 and not first:
                        if not isinstance(v, int) or v > 1:
                            sp.wait_ge(gained, v * SB - SB)
                        out_piece(v - 1)

            out_unit(0, first=True)
            out_unit(1)
            with sp.Fori(1, OUT_UNITS // 2) as i:
                out_unit(i * 2)
                out_unit(i * 2 + 1)
            sp.wait_ge(gained, (OUT_UNITS - 1) * SB)
            out_piece(OUT_UNITS - 1)
            for n, (lo, hi) in enumerate(STORES):
                sp.wait_ge(scaled_v, n + 1)
                sp.dma_start(out_rows[:, 0, lo:hi], xnew[:, 0, lo:hi]).then_inc(out_done, 16)
                sp.wait_ge(scaled_s, n + 1)
                sp.dma_start(out_rows[:, 1, lo:hi], xnew[:, 1, lo:hi]).then_inc(out_done, 16)
            sp.wait_ge(out_done, 2 * 16 * len(STORES))

        @block.gpsimd
        def _(pool):
            pool.memset(ident[:, :], 0.0).then_inc(ident_ready, 1)
            pool.wait_ge(ident_ready, 1)
            pool.affine_select(out=ident[:, :], in_=ident[:, :], compare_op=ALU.not_equal, fill=1.0, base=0,
                               pattern=[[-1, P]], channel_multiplier=1).then_inc(ident_ready, 1)
            for a, dq in ((0, 0), (1, P), (2, 0)):
                pool.iota(pos_t[:, a * P:(a + 1) * P], pattern=[[1, P]], base=dq, channel_multiplier=-1)
                pool.iota(pos_n[:, a * P:(a + 1) * P], pattern=[[-1, P]], base=dq, channel_multiplier=1).then_inc(pos_ready, 1)
            pool.memset(ones[:, :], 1.0)
            for h, s in enumerate(SLOPES):
                pool.memset(slope[:, h:h + 1], s)
            pool.memset(minus_half[:, :, :], -0.5).then_inc(ident_ready, 1)
            pool.wait_ge(ident_ready, 3)
            for s in range(SB):
                pool.wait_ge(x_squared, s + 1)
                pool.tensor_scalar(x_sum[:, s:s + 1], x_sum[:, s:s + 1], 1.0 / D, EPS, ALU.mult, ALU.add).then_inc(x_stat, 1)
                pool.wait_ge(x_stat, 3 * s + 1)
                pool.tensor_tensor(x_sum[:, s:s + 1], x_sum[:, s:s + 1], minus_half[:, 0, 0:1], ALU.pow).then_inc(x_stat, 1)
                pool.wait_ge(x_stat, 3 * s + 2)
                if s:
                    pool.wait_ge(x_turned, TPU)
                pool.tensor_scalar(diag[:, :], ident[:, :], x_sum[:, s:s + 1], None, ALU.mult).then_inc(x_stat, 1)

            def act_lo(i, n):
                pool.wait_ge(split_hi, n + 1)
                pool.tensor_tensor(act_split[:, bass.ds(i * TK, TK), S:2 * S], act_t[:, bass.ds(i * TK, TK), :],
                                   act_split[:, bass.ds(i * TK, TK), 0:S].bitcast(F32), ALU.subtract).then_inc(split_lo, 1)

            pool.wait_ge(x_turned, 2 * TPU)
            pool.memset(v_ones[:, :, :, P:VW], 1.0)
            pool.memset(attn[:, 0:4 * HG * S], 0.0)
            pool.memset(heads_in[:, :, :], 0.0).then_inc(zeroed, 1)

            def z_adds(j, u):
                for s in range(SB):
                    n = (u - NZ) * SB + s + 1
                    pool.wait_ge(z_part_taken, j * (NZ * SB) + n)
                    if isinstance(j, int) and j == 1:
                        pool.wait_ge(zeroed, 1)
                    else:
                        pool.wait_ge(z_summed, (j - 1) * (NZ * SB) + n)
                    total = z_sums[u][:, s * GW:(s + 1) * GW]
                    dst = z_set(u)[:, s * GW:(s + 1) * GW] if isinstance(j, int) and j == PHASES else total
                    pool.tensor_tensor(dst.rearrange("p (j e) -> p j e", j=HG), z_part[:, s, :, 0:P],
                                       total.rearrange("p (j e) -> p j e", j=HG), ALU.add).then_inc(z_summed, 1)

            def z_silu(u):
                pool.wait_ge(sigma_ready, u + 1)
                pool.tensor_tensor(z_set(u), z_set(u), z_sums[u], ALU.mult).then_inc(z_ready, 1)

            act_lo(0, 0)
            for u in range(NZ):
                z_adds(1, u)
            with pool.Fori(2, PHASES) as j:
                act_lo(j - 1, j - 1)
                for u in range(NZ):
                    z_adds(j, u)
            act_lo(PHASES - 1, PHASES - 1)
            pool.wait_ge(mod_summed, PHASES)
            pool.memset(ada_acc[:, :], 0.0).then_inc(zeroed, 1)
            for u in range(NZ):
                z_adds(PHASES, u)
                if u:
                    z_silu(u - 1)
            z_silu(NZ - 1)
            pool.wait_ge(z_ready, NZ)
            pool.memset(left[:, :, P:P + 1], 1.0)
            pool.memset(left[:, :, KEYS + 1:KEYS + 2], 1.0).then_inc(ones_set, 1)

            def group_rstd(g):
                pool.wait_ge(var_ready, g + 1)
                pool.tensor_tensor(rstd[:, :, :], sums[:, :, :], minus_half[:, :, :], ALU.pow).then_inc(rstd_ready, 1)

            with pool.Fori(0, GROUPS - 1) as g:
                group_rstd(g)
            for i in range(TPU - 2):
                act_lo(i, TPU + i)
            group_rstd(GROUPS - 1)
            act_lo(TPU - 2, 2 * TPU - 2)
            pool.wait_ge(tail_step, 2)
            pool.tensor_tensor(out_rstd[:, :], out_sum[:, :], minus_half[:, 0, :], ALU.pow).then_inc(out_rstd_ready, 1)

        @block.scalar
        def _(act):
            act.dma_start(vec_rows[0:KC, :], c.rearrange("o (k p) -> (o k) p", p=P)).then_inc(vec_ready, 16)
            act.dma_start(vec_rows[KC:2 * KC, :], g_norm.rearrange("l (k p) -> (l k) p", p=P)).then_inc(vec_ready, 16)
            act.dma_start(vec_rows[2 * KC:2 * KC + SB_HEADS, :], g_sb.rearrange("l (k p) -> (l k) p", p=P)).then_inc(vec_ready, 16)
            act.dma_start(vec_rows[2 * KC + SB_HEADS:3 * KC, :], g_dil.rearrange("l (k p) -> (l k) p", p=P)).then_inc(vec_ready, 16)
            act.dma_start(bias_rows[0:KC, :], b_ada[:, 0:D].rearrange("l (k p) -> (l k) p", p=P)).then_inc(vec_ready, 16)
            act.dma_start(bias_rows[KC:2 * KC, :], b_ada[:, D:2 * D].rearrange("l (k p) -> (l k) p", p=P)).then_inc(vec_ready, 16)
            act.dma_start(x_half, x_rows[:, 0, :]).then_inc(x_ready, 16)
            act.wait_ge(vec_copied, 1)
            act.activation(c_t[:, :], vec_t[:, 0:KC], ACT.Sigmoid).then_inc(c_sigma, 1)
            act.wait_ge(mask_step, MASK_STEPS)
            for s in range(SB):
                act.wait_ge(x_ready, 16 * (s + 1))
                act.activation(act_t[:, :, s * P:(s + 1) * P], x_half.rearrange("p (k e) -> p k e", k=KC), ACT.Square,
                               accum_out=x_sum[:, s:s + 1]).then_inc(x_squared, 1)
                act.wait_ge(x_squared, s + 1)
                for b in range(TPU):
                    act.wait_ge(x_turned, s * TPU + b + 1)
                    act.activation(act_t[:, b * TK:(b + 1) * TK, s * P:(s + 1) * P],
                                   acc[:, b % 4, :].rearrange("p (k e) -> p k e", k=TK), ACT.Copy).then_inc(x_copied, 1)
                if s == 0:
                    act.dma_start(x_half, x_rows[:, 1, :]).then_inc(x_ready, 16)

            def hi(slot, m, m1):
                act.activation(w_hi[:, m1, :, :].rearrange("p k e -> p (k e)"), ring[:, slot, :], ACT.Copy).then_inc(hi_ready, 1)

            def split(g, wide, t, i, ahead=False):
                done = g * (UNITS * (TPU - 1)) + TILES_FIRST - UNITS * (TPU - 1) + (UNITS if ahead else t) * (TPU - 1)
                if i >= 2:
                    act.wait_ge(tile_done, done + i - 1)
                elif i == 0:
                    act.wait_ge(tile_done, done)
                else:
                    act.wait_ge(acc_done, acc_before(g, t))
                n = (WIDE_ENTRIES if wide else NARROW_ENTRIES) if ahead else weight_entry(wide, t, i)
                entry_wait(act, g, wide, n)
                hi(n % RING, i, i % 2)

            def out_split(v, i):
                if i >= 2:
                    act.wait_ge(tile_done, v * (TPU - 1) + OUT_TILES + i - 1)
                elif i == 0:
                    act.wait_ge(tile_done, v * (TPU - 1) + OUT_TILES)
                else:
                    act.wait_ge(acc_done, v * SB + OUT_ACC)
                out_entry_wait(act, v, i)
                hi(i % RING, i, i % 2)

            def take(g, t):
                if t < 2:
                    dst = (q_t, k_t)[t]
                    for j in range(HG):
                        act.wait_ge(acc_done, acc_before(g, t) + j + 1)
                        act.activation(dst[:, j, :], acc[:, j, S:2 * S], ACT.Copy,
                                       scale=(INV_SQRT_D, 1.0)[t]).then_inc(cross_ready, 1)

            def h_hi(j):
                act.wait_ge(h_ready, j + 1)
                act.activation(act_split[:, bass.ds(j * TK, TK), 0:S], act_t[:, bass.ds(j * TK, TK), :], ACT.Copy).then_inc(split_hi, 1)

            def y_hi(i):
                if i == 0:
                    act.wait_ge(acc_done, OUT_ACC)
                act.wait_ge(y_taken, HG * (i + 1))
                act.activation(act_split[:, i * TK:(i + 1) * TK, 0:S], act_t[:, i * TK:(i + 1) * TK, :], ACT.Copy).then_inc(split_hi, 1)

            def probs_job(G, stick, j):
                act.wait_ge(scores_ready, G * HG + j + 1) if stick else None
                if stick:
                    if j >= 2:
                        act.wait_ge(probs_a, G * HG + j - 1)
                    act.activation(keep[:, j % 2, :], att[:, j, 0:KEYS], ACT.Sigmoid, scale=-1.0)
                    act.activation(probs[:, j, :], att[:, j, 0:KEYS], ACT.Sigmoid).then_inc(keep_ready, 1)
                else:
                    act.wait_ge(max_ready, G * HG - SB_HEADS + j + 1)
                    act.activation(probs[:, j, 0:P], probs[:, j, 0:P], ACT.Exp, bias=neg_max[:, j, 0:1])
                    act.activation(probs[:, j, P:KEYS], probs[:, j, P:KEYS], ACT.Exp, bias=neg_max[:, j, 1:2]).then_inc(probs_b, 1)

            def square_job(G, j):
                act.wait_ge(y_ready, G * HG + j + 1)
                for s in range(SB):
                    ins = act.activation(y_nat[:, j, s, :], att[:, j, s * VW:s * VW + P], ACT.Square,
                                         accum_out=sums[:, j, s:s + 1])
                ins.then_inc(y_squared, 1)

            def y_job(G, j):
                act.wait_ge(y_turned, G * HG + j // 2 * 2 + 2)
                act.activation(act_t[:, bass.ds(G * HG + j, 1), :].rearrange("p o s -> p (o s)"),
                               att[:, j // 2, (j % 2) * S:(j % 2 + 1) * S], ACT.Copy,
                               scale=vec_t[:, bass.ds(G * HG + j + 2 * KC, 1)]).then_inc(y_taken, 1)

            def job(G, stick, t, n):
                if t == 0 and n < HG:
                    probs_job(G, stick, n)
                elif t == 2 and n < 2:
                    square_job(G, 2 * n)
                    square_job(G, 2 * n + 1)
                elif t == 2 and n == TPU - 2:
                    for h in range(HG):
                        y_job(G, h)

            def multiplied(j, r):
                if ORDER[r][0] == "z":
                    act.wait_ge(z_part_done, j * (NZ * SB) + (r - Z0 + 1 - NZ) * SB)
                    return
                n = "qkv".index(ORDER[r][0]) + 1
                if isinstance(j, int) and j == PHASES:
                    act.wait_ge(acc_done, 2 * n)
                else:
                    act.wait_ge(tile_done, j * 3 + n - 3)

            def z_take(j, u, s):
                n = (u - NZ) * SB + s + 1
                act.wait_ge(z_part_done, j * (NZ * SB) + n)
                if not isinstance(j, int) or j > 1 or u:
                    act.wait_ge(z_summed, j * (NZ * SB) + n - SB)
                act.activation(z_part[:, s, :, 0:P], att[:, 2 + s, :].rearrange("p (j e) -> p j e", j=HG),
                               ACT.Copy).then_inc(z_part_taken, 1)

            def phase(j, par):
                h_hi(j - 1)
                for r in range(len(ORDER)):
                    if 0 <= r - 2 - Z0 < NZ:
                        z_take(j, r - 2 - Z0, 0)
                    if r >= 2:
                        multiplied(j, r - 2)
                    elif not isinstance(j, int) or j > 1:
                        multiplied(j - 1, len(ORDER) + r - 2)
                    if isinstance(j, int) and j == PHASES:
                        e = positions("w", LAST)[r]
                        last_wait(act, e)
                    else:
                        e = positions("w", PHASE)[r]
                        phase_wait(act, j, e)
                    hi(e % RING, r, (r + 1 + par) % 2)
                    if 0 <= r - 2 - Z0 < NZ:
                        z_take(j, r - 2 - Z0, 1)
                    if isinstance(j, int) and j == PHASES and r == 2:
                        act.wait_ge(zeroed, 2)
                        act.dma_start(ada_acc[0:1, :], b_ada[:, 2 * D:3 * D]).then_inc(gate_seeded, 16)
                    if isinstance(j, int) and j == PHASES and 0 <= r - 3 - Z0 < NZ:
                        z_sigma(r - 3 - Z0)

            def z_sigma(u):
                act.wait_ge(z_summed, (NZ * (PHASES - 1) + u + 1) * SB)
                act.activation(z_sums[u], z_set(u), ACT.Sigmoid).then_inc(sigma_ready, 1)

            phase(1, 1)
            with act.Fori(1, PHASES // 2) as i:
                phase(i * 2, 0)
                phase(i * 2 + 1, 1)
            phase(PHASES, 0)
            act.wait_ge(acc_done, 4)
            act.wait_ge(raw_ready[0], landed(PROJ_BASE))
            hi(0, 0, 0)
            z_sigma(NZ - 1)
            act.wait_ge(ones_set, 1)

            def group(g, wide, stick):
                G = g - 1
                for t in range(UNITS):
                    for i in range(TPU):
                        if t or i:
                            split(g, wide, t, i)
                        if t and i == 0:
                            take(g, t - 1)
                        if i >= 1:
                            job(G, stick, t, i - 1)
                split(g, wide, 0, 0, ahead=True)

            with act.Fori(1, WIDE_GROUPS) as g:
                group(g, True, True)
            with act.Fori(WIDE_GROUPS, GROUPS) as g:
                group(g, False, False)

            G = GROUPS - 1
            for i in range(TPU):
                if i:
                    out_split(0, i)
                if i == 1:
                    for j in range(HG):
                        probs_job(G, False, j)
                if i < 3:
                    y_hi(2 * i)
                    y_hi(2 * i + 1)
                if i == 4:
                    y_hi(TPU - 2)
                if i == 5:
                    for j in range(HG):
                        square_job(G, j)
            for j in range(HG):
                y_job(G, j)
            y_hi(TPU - 1)

            def gate_copy(v, par):
                act.wait_ge(gate_ready, v + 1)
                act.wait_ge(acc_taken, v * SB + OUT_ACC - SB)
                act.activation(gate_row[:, par, :], att[:, 2 + par, :], ACT.Copy).then_inc(gate_copied, 1)

            def square_res(v):
                for s in range(SB):
                    act.wait_ge(res_ready, v * SB + s + 1)
                    act.activation(squares[:, s, :], res[:, s, :], ACT.Square,
                                   accum_out=out_sums[:, s, bass.ds(v, 1)]).then_inc(res_squared, 1)

            def out_unit(v, par):
                for i in range(TPU):
                    out_split(v, i)
                    if i == 0:
                        gate_copy(v - 1, 1 - par)
                    if i == 3:
                        square_res(v - 1)

            out_unit(1, 1)
            with act.Fori(1, OUT_UNITS // 2) as i:
                out_unit(i * 2, 0)
                out_unit(i * 2 + 1, 1)
            gate_copy(OUT_UNITS - 1, 1)
            square_res(OUT_UNITS - 1)
            act.wait_ge(out_rstd_ready, 1)
            for lo, hi in STORES:
                act.activation(xnew[:, 1, lo:hi], xnew[:, 1, lo:hi],
                               ACT.Copy, scale=out_rstd[:, 1:2]).then_inc(scaled_s, 1)

        @block.vector
        def _(dve):
            dve.wait_ge(pos_ready, 3)
            steps = [0]

            def step(ins):
                ins.then_inc(mask_step, 1)
                steps[0] += 1
                dve.wait_ge(mask_step, steps[0])

            low4, low16 = tmp[0].bitcast(I32), tmp[1].bitcast(I32)
            f0, f1 = tmp[2], tmp[3]
            step(dve.tensor_scalar(low4, pos_t, 3, None, ALU.bitwise_and))
            step(dve.tensor_scalar(low16, pos_t, 15, None, ALU.bitwise_and))
            step(dve.tensor_scalar(f0, low4, 0.0, None, ALU.is_equal))
            step(dve.scalar_tensor_tensor(f1, low16, 0.0, f0, ALU.is_equal, ALU.add))
            step(dve.scalar_tensor_tensor(f0, pos_t, float(WINDOW), f1, ALU.is_le, ALU.add))
            step(dve.scalar_tensor_tensor(count_t[:, :], pos_t, 0.0, f0, ALU.is_ge, ALU.mult))
            step(dve.tensor_scalar(causal_t[:, :], pos_t, 0.0, None, ALU.is_gt))
            step(dve.tensor_scalar(stop_mask[:, :], pos_n, 0.0, None, ALU.is_le))
            step(dve.tensor_scalar(low4, pos_n, 3, None, ALU.bitwise_and))
            step(dve.tensor_scalar(f0, low4, 0.0, None, ALU.is_equal))
            step(dve.scalar_tensor_tensor(f1, pos_n, float(WINDOW), f0, ALU.is_le, ALU.max))
            step(dve.scalar_tensor_tensor(f0, pos_n, 0.0, f1, ALU.is_ge, ALU.mult))
            step(dve.tensor_scalar(f1, f0, -MASKED, MASKED, ALU.mult, ALU.add))
            step(dve.tensor_tensor(dist_mask[:, :], f1, pos_n, ALU.subtract))

            assert steps[0] == MASK_STEPS

            dve.wait_ge(vec_turned, 1)
            for a in range(2):
                dve.tensor_copy(bias_t[:, :, a, :], att[:, 1, a * KC:(a + 1) * KC].rearrange("p (j k) -> p j k", k=TK))
            dve.tensor_copy(vec_t[:, :], att[:, 0, 0:3 * KC]).then_inc(vec_copied, 1)
            dve.wait_ge(c_sigma, 1)
            dve.wait_ge(vec_copied, 1)
            dve.tensor_tensor(c_t[:, :], c_t[:, :], vec_t[:, 0:KC], ALU.mult).then_inc(c_ready, 1)
            dve.wait_ge(c_ready, 1)

            def ada(slot, j, par, n):
                for kk in range(TK):
                    cols = mod_acc[:, par, kk % 2, n % 2, :]
                    w = ring[:, slot, kk * GW:(kk + 1) * GW]
                    k = n // 2 * TK + kk
                    if kk >= 2:
                        dve.wait_ge(mod_part, j * (2 * ADA_TILES) + 2 * n + kk - 1)
                    if n < 2 and kk < 2:
                        ins = dve.tensor_scalar(cols, w, c_t[:, k:k + 1], None, ALU.mult)
                    else:
                        ins = dve.scalar_tensor_tensor(cols, w, c_t[:, k:k + 1], cols, ALU.mult, ALU.add)
                    if kk < 2:
                        ins.then_inc(mod_part, 1)
                ins.then_inc(ring_used, 1)

            def lo(slot, par):
                dve.tensor_tensor(w_lo[:, par, :, :].rearrange("p k e -> p (k e)"), ring[:, slot, :],
                                  w_hi[:, par, :, :].rearrange("p k e -> p (k e)").bitcast(F32), ALU.subtract).then_inc(ring_used, 1)

            def modulate(j):
                dve.wait_ge(mod_summed, j + 1)
                dve.tensor_tensor(mod_t[:, :, :], att[:, 3, 0:2 * TK].rearrange("p (a k) -> p a k", a=2),
                                  bias_t[:, bass.ds(j, 1), :, :].rearrange("p o a k -> p (o a) k"), ALU.add).then_inc(mod_ready, 1)
                dve.wait_ge(mod_ready, j * 2 + 1)
                dve.scalar_tensor_tensor(mul_t[:, :], mod_t[:, 1, :], 1.0, vec_t[:, bass.ds(j * TK + KC, TK)],
                                         ALU.add, ALU.mult).then_inc(mod_ready, 1)
                dve.wait_ge(mod_ready, j * 2 + 2)
                for k in range(TK):
                    chunk = act_t[:, bass.ds(j * TK + k, 1), :].rearrange("p o s -> p (o s)")
                    ins = dve.tensor_scalar(chunk, chunk, mul_t[:, k:k + 1], mod_t[:, 0, k:k + 1], ALU.mult, ALU.add)
                ins.then_inc(h_ready, 1)

            def split(g, wide, t, i, ahead=False):
                m = UNITS * TPU if ahead else t * TPU + i
                dve.wait_ge(hi_ready, g * (UNITS * TPU) + W_FIRST - UNITS * TPU + m + 1)
                n = (WIDE_ENTRIES if wide else NARROW_ENTRIES) if ahead else weight_entry(wide, t, i)
                lo(n % RING, i % 2)

            for n in range(ADA_TILES):
                dve.wait_ge(raw_ready[n % RING], 16 * (n // RING + 1))
                if n >= 2:
                    dve.wait_ge(ring_used, n - 1)
                ada(n % RING, 0, 0, n)
            dve.wait_ge(x_copied, 2 * TPU)

            def phase(j, par):
                n = r = 0
                for e, kind in enumerate(PHASE):
                    if kind == "a":
                        phase_wait(dve, j, e)
                        if n >= 2:
                            dve.wait_ge(ring_used, j * PHASE_USES + FIRST_ENTRIES - PHASE_USES + e - 1)
                        ada(e % RING, j, par, n)
                        n += 1
                        if n == 4:
                            modulate(j - 1)
                    else:
                        dve.wait_ge(hi_ready, j * len(ORDER) + r + 1 - len(ORDER))
                        lo(e % RING, (r + 1 + par) % 2)
                        r += 1

            with dve.Fori(0, (PHASES - 1) // 2) as i:
                phase(i * 2 + 1, 1)
                phase(i * 2 + 2, 0)
            phase(PHASES - 1, 1)
            modulate(PHASES - 1)

            def gate_tile(slot, k, half):
                cols = ada_acc[:, half * (D // 2):(half + 1) * (D // 2)]
                dve.scalar_tensor_tensor(cols, ring[:, slot, :], c_t[:, bass.ds(k, 1)], cols, ALU.mult, ALU.add).then_inc(ring_used, 1)

            nw = ng = 0
            for e, kind in enumerate(LAST):
                if kind == "w":
                    dve.wait_ge(hi_ready, (PHASES - 1) * len(ORDER) + nw + 1)
                    lo(e % RING, (nw + 1) % 2)
                    nw += 1
                else:
                    if ng == 0:
                        dve.wait_ge(gate_seeded, 16)
                    if ng >= 2:
                        dve.wait_ge(ring_used, LAST_USES + e - 1)
                    last_wait(dve, e)
                    gate_tile(e % RING, ng // 2, ng % 2)
                    ng += 1
            dve.wait_ge(z_ready, 2)
            dve.wait_ge(acc_done, 2)
            for b in range(2):
                dve.tensor_scalar(q_t[:, 2 * b:2 * b + 2, :].rearrange("p j s -> p (j s)"), acc[:, b, :], INV_SQRT_D, None,
                                  ALU.mult).then_inc(acc_taken, 1)
            dve.wait_ge(acc_done, 4)
            for b in range(2):
                dve.tensor_copy(k_t[:, 2 * b:2 * b + 2, :].rearrange("p j s -> p (j s)"), acc[:, 2 + b, :]).then_inc(acc_taken, 1)
            dve.wait_ge(hi_ready, W_FIRST + 1)
            lo(0, 0)
            dve.wait_ge(ones_set, 1)
            for s in range(SB):
                dve.wait_ge(acc_done, 4 + s + 1)
                dve.tensor_copy(v_ones[:, s, :, 0:P], att[:, s, :].rearrange("p (j e) -> p j e", j=HG)).then_inc(acc_taken, 1)

            def out_split(v, i):
                dve.wait_ge(hi_ready, v * TPU + W_FIRST + (GROUPS - 1) * UNITS * TPU + i + 1)
                lo(i % RING, i % 2)

            def gate(g, wide, t, m):
                n = unit_entry(wide, t) + gates_at(wide, t)[m]
                i = sum(len(gates_at(wide, u)) for u in range(t)) + m
                entry_wait(dve, g, wide, n)
                first = (GATE_WIDE, GATE_LAST - GATE_WIDE) if wide else (
                    GATE_NARROW, GATE_BASE_NARROW - WIDE_GROUPS * GATE_NARROW)
                gate_tile(n % RING, g * first[0] + first[1] + i // 2, i % 2)

            def take(g, t):
                if t < 2:
                    dst = (q_t, k_t)[t]
                    for j in range(HG):
                        dve.wait_ge(cross_ready, g * (2 * HG) + t * HG + j + 1 - 2 * HG)
                        if t == 0:
                            dve.scalar_tensor_tensor(dst[:, j, :], acc[:, j, 0:S], INV_SQRT_D, dst[:, j, :],
                                                     ALU.mult, ALU.add).then_inc(acc_taken, 1)
                        else:
                            dve.tensor_tensor(dst[:, j, :], acc[:, j, 0:S], dst[:, j, :], ALU.add).then_inc(acc_taken, 1)
                else:
                    for s in range(SB):
                        dve.wait_ge(acc_done, acc_before(g, t) + s + 1)
                        dve.tensor_copy(v_ones[:, s, :, 0:P], acc[:, s, :].rearrange("p (j e) -> p j e", j=HG)).then_inc(acc_taken, 1)

            def probs_job(G, stick, j):
                if stick:
                    dve.wait_ge(keep_ready, G * HG + j + 1)
                    dve.tensor_tensor_scan(left[:, j % 2, 0:P][:, ::-1], keep[:, j % 2, 0:P][:, ::-1],
                                           stop_mask[:, 0:P][:, ::-1], 1.0, ALU.mult, ALU.max)
                    dve.tensor_tensor_scan(left[:, j % 2, P + 1:KEYS + 1][:, ::-1], keep[:, j % 2, P:KEYS][:, ::-1],
                                           stop_mask[:, P:KEYS][:, ::-1], 1.0, ALU.mult, ALU.max).then_inc(left_ready, 1)
                    dve.wait_ge(left_ready, G * HG + j + 1)
                    dve.tensor_tensor(probs[:, j, 0:P], probs[:, j, 0:P], left[:, j % 2, 1:P + 1], ALU.mult)
                    dve.tensor_tensor(probs[:, j, P:KEYS], probs[:, j, P:KEYS], left[:, j % 2, P + 2:KEYS + 2],
                                      ALU.mult).then_inc(probs_a, 1)
                else:
                    n = G * HG - SB_HEADS + j
                    dve.wait_ge(scores_ready, G * HG + j + 1)
                    dve.scalar_tensor_tensor(probs[:, j, :], dist_mask[:, :], slope[:, bass.ds(n, 1)], att[:, j, 0:KEYS],
                                             ALU.mult, ALU.add).then_inc(biased, 1)
                    dve.wait_ge(biased, n + 1)
                    dve.tensor_reduce(neg_max[:, j, 0:1], probs[:, j, 0:P], AX.X, ALU.max, negate=True)
                    dve.tensor_reduce(neg_max[:, j, 1:2], probs[:, j, P:KEYS], AX.X, ALU.max, negate=True).then_inc(max_ready, 1)

            def turned_job(G, stick, j):
                dve.wait_ge(probs_turned, G * HG + j + 1)
                dve.tensor_tensor(probs_t[:, j, :], att[:, j, 0:KEYS], (causal_t if stick else count_t)[:, :],
                                  ALU.mult).then_inc(probs_t_ready, 1)

            def variance_job(G, stick):
                dve.wait_ge(y_squared, G * HG + HG)
                if stick:
                    dve.tensor_scalar(sums[:, :, :], sums[:, :, :], 1.0 / P, EPS, ALU.mult, ALU.add).then_inc(var_ready, 1)
                    return
                n = G * 2 - 2 * SB_GROUPS
                for s in range(SB):
                    ins = dve.tensor_copy(dens[:, :, s:s + 1], att[:, :, s * VW + P:s * VW + P + 1])
                ins.then_inc(den_step, 1)
                dve.wait_ge(den_step, n + 1)
                dve.scalar_tensor_tensor(den_sq[:, :, :], dens[:, :, :], EPS, dens[:, :, :], ALU.mult, ALU.mult).then_inc(den_step, 1)
                dve.wait_ge(den_step, n + 2)
                dve.scalar_tensor_tensor(sums[:, :, :], sums[:, :, :], 1.0 / P, den_sq[:, :, :], ALU.mult, ALU.add).then_inc(var_ready, 1)

            def norm_job(G, j):
                if j == 0:
                    dve.wait_ge(rstd_ready, G + 1)
                for s in range(SB):
                    at = s * GW + j * P
                    z = act_t[:, bass.ds(G * TK + at // S, 1), at % S:at % S + P].rearrange("p o e -> p (o e)")
                    ins = dve.scalar_tensor_tensor(y_nat[:, j, s, :], att[:, j, s * VW:s * VW + P], rstd[:, j, s:s + 1],
                                                   z, ALU.mult, ALU.mult)
                ins.then_inc(y_normed, 1)

            def job(G, stick, t, n):
                if t == 0 and n < HG:
                    probs_job(G, stick, n)
                elif t == 1 and n < HG:
                    turned_job(G, stick, n)
                elif t == 2 and n == 2:
                    variance_job(G, stick)
                elif t == 2 and n in (3, 4):
                    norm_job(G, 2 * n - 6)
                    norm_job(G, 2 * n - 5)

            def group(g, wide, stick):
                G = g - 1
                for t in range(UNITS):
                    m = 0
                    for i in range(TPU):
                        if t or i:
                            split(g, wide, t, i)
                        if t and i == 0:
                            take(g, t - 1)
                        if i >= 1:
                            job(G, stick, t, i - 1)
                        while m < len(gates_at(wide, t)) and (
                                i == TPU - 1 or weight_entry(wide, t, i + 1) > unit_entry(wide, t) + gates_at(wide, t)[m]):
                            gate(g, wide, t, m)
                            m += 1
                split(g, wide, 0, 0, ahead=True)
                take(g, 2)

            with dve.Fori(1, WIDE_GROUPS) as g:
                group(g, True, True)
            with dve.Fori(WIDE_GROUPS, GROUPS) as g:
                group(g, False, False)

            G = GROUPS - 1
            for i in range(TPU):
                if i:
                    out_split(0, i)
                if i == 1:
                    for j in range(HG):
                        probs_job(G, False, j)
                if i == 3:
                    for j in range(HG):
                        turned_job(G, False, j)
                if i == 5:
                    variance_job(G, False)
                    for j in range(HG):
                        norm_job(G, j)
            dve.wait_ge(split_hi, 2 * TPU)
            dve.wait_ge(split_lo, 2 * TPU - 1)
            k = (TPU - 1) * TK
            dve.tensor_tensor(act_split[:, k:KC, S:2 * S], act_t[:, k:KC, :], act_split[:, k:KC, 0:S].bitcast(F32),
                              ALU.subtract).then_inc(split_lo, 1)

            def finish(v, par):
                dve.wait_ge(gate_copied, v + 1)
                dve.wait_ge(xg_ready, v * 32 + 32)
                if not isinstance(v, int) or v:
                    dve.wait_ge(res_squared, v * SB)
                    dve.wait_ge(gained, v * SB)
                cols = bass.ds(v * GW, GW)
                for s in range(SB):
                    dve.wait_ge(acc_done, v * SB + OUT_ACC + s + 1)
                    dve.tensor_tensor(res[:, s, :], acc[:, 2 * par + s, :], gate_row[:, par, :], ALU.mult).then_inc(acc_taken, 1)
                for s in range(SB):
                    dve.wait_ge(acc_taken, v * SB + OUT_ACC + s + 1)
                    dve.tensor_tensor(res[:, s, :], res[:, s, :], xnew[:, s, cols], ALU.add).then_inc(res_ready, 1)
                for s in range(SB):
                    dve.wait_ge(res_ready, v * SB + s + 1)
                    dve.tensor_tensor(xnew[:, s, cols], res[:, s, :], g_final_row[:, :], ALU.mult).then_inc(gained, 1)

            def out_unit(v, par):
                for i in range(TPU):
                    out_split(v, i)
                    if i == 1:
                        finish(v - 1, 1 - par)

            out_unit(1, 1)
            with dve.Fori(1, OUT_UNITS // 2) as i:
                out_unit(i * 2, 0)
                out_unit(i * 2 + 1, 1)
            finish(OUT_UNITS - 1, 1)
            dve.wait_ge(res_squared, OUT_UNITS * SB)
            dve.reduce_sum(out_sum[:, :], out_sums[:, :, :], AX.X).then_inc(tail_step, 1)
            dve.wait_ge(tail_step, 1)
            dve.tensor_scalar(out_sum[:, :], out_sum[:, :], 1.0 / D, EPS, ALU.mult, ALU.add).then_inc(tail_step, 1)
            dve.wait_ge(out_rstd_ready, 1)
            dve.wait_ge(gained, OUT_UNITS * SB)
            for lo, hi in STORES:
                dve.tensor_scalar(xnew[:, 0, lo:hi], xnew[:, 0, lo:hi], out_rstd[:, 0:1], None, ALU.mult).then_inc(scaled_v, 1)

        @block.tensor
        def _(pe):
            pe.wait_ge(ident_ready, 3)
            pe.wait_ge(vec_ready, 96)
            pe.transpose(att[:, 1, 0:2 * KC], bias_rows[:, :], ident[0:2 * KC, 0:2 * KC])
            pe.transpose(att[:, 0, 0:3 * KC], vec_rows[:, :], ident[0:3 * KC, 0:3 * KC]).then_inc(vec_turned, 1)
            for s in range(SB):
                pe.wait_ge(x_stat, 3 * (s + 1))
                for b in range(TPU):
                    n = s * TPU + b
                    if n >= 4:
                        pe.wait_ge(x_copied, n - 3)
                    for k in range(TK):
                        kc = b * TK + k
                        mm = pe.matmul(acc[:, b % 4, k * P:(k + 1) * P], x_half[:, kc * P:(kc + 1) * P], diag[:, :],
                                       start=True, stop=True)
                    mm.then_inc(x_turned, 1)
            def turned_tile(i, w, last):
                for kk in range(TK):
                    k = i * TK + kk
                    for e in range(HG):
                        pe.matmul(acc[:, e, :], w_hi[:, w, kk, e * P:(e + 1) * P], act_split[:, k, :],
                                  start=(k == 0), stop=False, skip_group_check=True)
                        mm = pe.matmul(acc[:, e, 0:S], w_lo[:, w, kk, e * P:(e + 1) * P], act_split[:, k, 0:S],
                                       start=False, stop=(k == KC - 1), skip_group_check=True)
                        if last and kk == TK - 1:
                            mm.then_inc(acc_done, 1)
                if not last:
                    mm.then_inc(tile_done, 1)

            def rows_tile(i, w, last, bank):
                for kk in range(TK):
                    k = i * TK + kk
                    for s in range(SB):
                        a_hi = act_split[:, k, s * P:(s + 1) * P]
                        a_lo = act_split[:, k, S + s * P:S + (s + 1) * P]
                        pe.matmul(acc[:, bank + s, :], a_hi, w_hi[:, w, kk, :], start=(k == 0), stop=False)
                        pe.matmul(acc[:, bank + s, :], a_hi, w_lo[:, w, kk, :], start=False, stop=False)
                        mm = pe.matmul(acc[:, bank + s, :], a_lo, w_hi[:, w, kk, :], start=False, stop=(k == KC - 1))
                        if last and kk == TK - 1:
                            mm.then_inc(acc_done, 1)
                if not last:
                    mm.then_inc(tile_done, 1)

            def packed_tile(i, w, first_bank, last):
                for kk in range(TK):
                    k = i * TK + kk
                    for e in range(HG):
                        dst = acc[:, first_bank + e // 2, (e % 2) * S:(e % 2 + 1) * S]
                        w_h, w_l = (a[:, w, kk, e * P:(e + 1) * P] for a in (w_hi, w_lo))
                        pe.matmul(dst, w_h, act_split[:, k, 0:S], start=(k == 0 and e % 2 == 0), stop=False, skip_group_check=True)
                        pe.matmul(dst, w_h, act_split[:, k, S:2 * S], start=False, stop=False, skip_group_check=True)
                        mm = pe.matmul(dst, w_l, act_split[:, k, 0:S], start=False, stop=(k == KC - 1), skip_group_check=True)
                        if last and kk == TK - 1 and e % 2 == 1:
                            mm.then_inc(acc_done, 1)
                if not last:
                    mm.then_inc(tile_done, 1)

            def phase_tile(j, r):
                i, w = j - 1, (j + r + 1) % 2
                if j < PHASES:
                    pe.wait_ge(ring_used, FIRST_ENTRIES + (j - 1) * PHASE_USES + positions("w", PHASE)[r] + 1)
                else:
                    pe.wait_ge(ring_used, LAST_USES + positions("w", LAST)[r] + 1)
                if r == 0:
                    pe.wait_ge(split_lo, j)
                t = ORDER[r][0]
                if t in "qk":
                    packed_tile(i, w, 2 * "qk".index(t), i == TPU - 1)
                    return
                for s in range(SB):
                    if t == "z" and (j > 1 or r > Z0):
                        pe.wait_ge(z_part_taken, ((j - 1) * NZ + r - Z0 - 1) * SB + s + 1)
                    for kk in range(TK):
                        k = i * TK + kk
                        a_hi = act_split[:, k, s * P:(s + 1) * P]
                        a_lo = act_split[:, k, S + s * P:S + (s + 1) * P]
                        dst = att[:, (2 if t == "z" else 0) + s, :]
                        begin, end = (k == 0, k == KC - 1) if t == "v" else (kk == 0, kk == TK - 1)
                        pe.matmul(dst, a_hi, w_hi[:, w, kk, :], start=begin, stop=False)
                        pe.matmul(dst, a_hi, w_lo[:, w, kk, :], start=False, stop=False)
                        mm = pe.matmul(dst, a_lo, w_hi[:, w, kk, :], start=False, stop=end)
                    if t == "z":
                        mm.then_inc(z_part_done, 1)
                    elif i == TPU - 1:
                        mm.then_inc(acc_done, 1)
                if t == "v" and i < TPU - 1:
                    mm.then_inc(tile_done, 1)

            def column_sums(j):
                pe.wait_ge(ring_used, FIRST_ENTRIES + (j * PHASE_USES - 1 if j else 0))
                if j:
                    pe.wait_ge(z_part_taken, j * NZ * SB)
                for a in range(2):
                    for k in range(TK):
                        for kk in range(2):
                            mm = pe.matmul(att[:, 3, a * TK + k:a * TK + k + 1], mod_acc[:, j % 2, kk, a, k * P:(k + 1) * P],
                                           ones[:, 0:1], start=(kk == 0), stop=(kk == 1))
                mm.then_inc(mod_summed, 1)

            column_sums(0)
            for j in range(1, PHASES):
                for r in range(len(ORDER) - 1):
                    phase_tile(j, r)
                column_sums(j)
                phase_tile(j, len(ORDER) - 1)
            for r in range(len(ORDER)):
                phase_tile(PHASES, r)

            def unit(g, wide, t):
                if t == 0:
                    pe.wait_ge(acc_taken, acc_before(g, 0))
                elif t == 1:
                    pe.wait_ge(acc_taken, acc_before(g, 1))
                else:
                    pe.wait_ge(acc_taken, acc_before(g, 1) + SB)
                for i in range(TPU):
                    if t == 2 and i == TPU - 1:
                        turn_y(g - 1)
                    pe.wait_ge(ring_used, group_uses(g, wide) + weight_entry(wide, t, i) + 1)
                    if t < 2:
                        turned_tile(i, i % 2, i == TPU - 1)
                    else:
                        rows_tile(i, i % 2, i == TPU - 1, 0)

            def scores(g):
                if isinstance(g, int):
                    pe.wait_ge(acc_taken, ACC_FIRST)
                    pe.wait_ge(z_part_taken, NZ * SB * PHASES)
                else:
                    pe.wait_ge(acc_taken, acc_before(g, 2))
                    pe.wait_ge(y_taken, g * HG)
                for j in range(HG):
                    pe.matmul(att[:, j, 0:P], q_t[:, j, 0:P], k_t[:, j, 0:P], start=True, stop=True)
                    pe.matmul(att[:, j, P:KEYS], q_t[:, j, P:S], k_t[:, j, :], start=True, stop=True).then_inc(scores_ready, 1)

            def turn_probs(G, stick):
                for j in range(HG):
                    if stick:
                        pe.wait_ge(probs_a, G * HG + j + 1)
                    else:
                        pe.wait_ge(probs_b, G * HG - SB_HEADS + j + 1)
                    for b in range(3):
                        mm = pe.transpose(att[:, j, b * P:(b + 1) * P], probs[:, j, b * P:(b + 1) * P], ident[:, :])
                    mm.then_inc(probs_turned, 1)

            def values(G):
                for j in range(HG):
                    pe.wait_ge(probs_t_ready, G * HG + j + 1)
                    pe.matmul(att[:, j, 0:VW], probs_t[:, j, 0:P], v_ones[:, 0, j, :], start=True, stop=True)
                    pe.matmul(att[:, j, VW:2 * VW], probs_t[:, j, P:2 * P], v_ones[:, 0, j, :], start=True, stop=False)
                    pe.matmul(att[:, j, VW:2 * VW], probs_t[:, j, 2 * P:KEYS], v_ones[:, 1, j, :], start=False, stop=True).then_inc(y_ready, 1)

            def turn_y(G):
                pe.wait_ge(y_normed, G * HG + HG)
                for j in range(HG):
                    for s in range(SB):
                        mm = pe.transpose(att[:, j // 2, (j % 2) * S + s * P:(j % 2) * S + (s + 1) * P], y_nat[:, j, s, :], ident[:, :])
                    mm.then_inc(y_turned, 1)

            def group(g, wide, stick):
                unit(g, wide, 0)
                turn_probs(g - 1, stick)
                unit(g, wide, 1)
                values(g - 1)
                unit(g, wide, 2)
                scores(g)

            scores(0)
            pe.wait_ge(ones_set, 1)
            with pe.Fori(1, WIDE_GROUPS) as g:
                group(g, True, True)
            with pe.Fori(WIDE_GROUPS, GROUPS) as g:
                group(g, False, False)

            G = GROUPS - 1

            def out_unit(v, par, first=False):
                pe.wait_ge(acc_taken, OUT_ACC if first else v * SB + OUT_ACC - SB)
                for i in range(TPU):
                    if first and i == 3:
                        turn_probs(G, False)
                    if first and i == 4:
                        values(G)
                    if first and i == 6:
                        turn_y(G)
                    if i == TPU - 1:
                        if not first:
                            pe.wait_ge(gate_copied, v - 1) if not isinstance(v, int) or v > 1 else None
                        pe.matmul(att[:, 2 + par, :], ones[:, :], ada_acc[:, bass.ds(v * GW, GW)], start=True, stop=True).then_inc(gate_ready, 1)
                    pe.wait_ge(ring_used, v * TPU + OUT_BASE - SKIPPED + i + 1)
                    if first:
                        pe.wait_ge(split_lo, TPU + i + 1)
                    rows_tile(i, i % 2, i == TPU - 1, 2 * par)

            out_unit(0, 0, first=True)
            out_unit(1, 1)
            with pe.Fori(1, OUT_UNITS // 2) as i:
                out_unit(i * 2, 0)
                out_unit(i * 2 + 1, 1)


_INS = ["x", "c", "w_ada", "b_ada", "g_norm", "w_in", "g_sb", "g_dil", "w_out", "g_final"]


def kernel(**inputs):
    import concourse.bacc as bacc
    from concourse.bass_utils import run_bass_kernel_spmd

    nc = bacc.Bacc("TRN2", target_bir_lowering=False, num_devices=1, dynamic_dma_scratch_size=1024)
    arrays, args = {}, []
    for name in _INS:
        a = np.ascontiguousarray(inputs[name])
        arrays[f"in_{name}"] = a
        args.append(nc.dram_tensor(f"in_{name}", a.shape, mybir.dt.from_np(a.dtype), kind="ExternalInput").ap())
    shape = inputs["x"].shape
    args.append(nc.dram_tensor("out", shape, F32, kind="ExternalOutput").ap())
    build(nc, *args)
    r = run_bass_kernel_spmd(nc, [arrays], core_ids=[0])
    return r.results[0]["out"]
```

```python
from contextlib import ExitStack

import numpy as np
import concourse.bass as bass
from concourse import mybir

F32 = mybir.dt.float32
F32R = mybir.dt.float32r
BF16 = mybir.dt.bfloat16
I32 = mybir.dt.int32
ALU = mybir.AluOpType
ACT = mybir.ActivationFunctionType
AX = mybir.AxisListType

P = 128
S = 256
SB = S // P
D = 4096
KC = D // P
HEADS = 32
SB_HEADS = 16
HG = 4
GW = HG * P
GROUPS = HEADS // HG
SB_GROUPS = SB_HEADS // HG
PARTS = 4
TK = 4
TPU = KC // TK
TILE = TK * GW
RING = 4
PHASES = D // GW
ADA_TILES = 2 * TPU
ORDER = [("q", 0)] + [("z", G) for G in range(1, GROUPS)] + [("z", 0), ("k", GROUPS - 1), ("k", 0), ("v", 0)]
U0, NS = 1, GROUPS + 1
SUMMED = ORDER[U0:U0 + NS]
NZ = GROUPS
PHASE = "a" * (ADA_TILES - len(ORDER) + 1) + "w" + "aw" * (len(ORDER) - 1)
LAST = "wwwwgwwgwwgwwgww"
FIRST_ENTRIES = ADA_TILES
PHASE_ENTRIES = len(PHASE)
LAST_BASE = FIRST_ENTRIES + (PHASES - 1) * PHASE_ENTRIES
assert PHASE.count("a") == ADA_TILES and PHASE.count("w") == LAST.count("w") == len(ORDER)
WIDE_GROUPS = SB_GROUPS + 1
UNITS = {"wide": "qkv", "narrow": "qkv", "final": "qv"}
GATES = {"wide": [[2, 5, 8, 11]] * 3, "narrow": [[3, 8], [4], [4]], "final": [[3, 8], [3, 8]]}
ENTRIES = {kind: len(UNITS[kind]) * TPU + sum(len(u) for u in GATES[kind]) for kind in UNITS}
OUT_UNITS = D // GW
PROJ_BASE = LAST_BASE + len(LAST)
NARROW_BASE = PROJ_BASE + (WIDE_GROUPS - 1) * ENTRIES["wide"]
OUT_BASE = NARROW_BASE + (GROUPS - 1 - WIDE_GROUPS) * ENTRIES["narrow"] + ENTRIES["final"]
GROUP_BASE = {"wide": PROJ_BASE - ENTRIES["wide"], "narrow": NARROW_BASE - WIDE_GROUPS * ENTRIES["narrow"],
              "final": OUT_BASE - GROUPS * ENTRIES["final"]}
assert all(n % RING == 0 for n in (FIRST_ENTRIES, PHASE_ENTRIES, len(LAST), *ENTRIES.values()))
GATE_CHUNKS = {kind: sum(len(u) for u in GATES[kind]) // 2 for kind in GATES}
GATE_NARROW = LAST.count("g") // 2 + (WIDE_GROUPS - 1) * GATE_CHUNKS["wide"]
GATE_BASE = {"wide": LAST.count("g") // 2 - GATE_CHUNKS["wide"], "narrow": GATE_NARROW - WIDE_GROUPS * GATE_CHUNKS["narrow"],
             "final": KC - GROUPS * GATE_CHUNKS["final"]}
assert GATE_NARROW + (GROUPS - 1 - WIDE_GROUPS) * GATE_CHUNKS["narrow"] + GATE_CHUNKS["final"] == KC
KEYS = 3 * P
VW = P + 1
EPS = 1e-6
INV_SQRT_D = float(P) ** -0.5
SLOPES = [2.0 ** (-8.0 * (h + 1) / (HEADS - SB_HEADS)) for h in range(HEADS - SB_HEADS)]
MASKED = -1.0e30
WINDOW = 128
ACC_PER_GROUP = 2 * HG + SB
ACC_AT = [0, HG, 2 * HG]
ACC_FINAL = HG + SB
ACC_FIRST = 2 * 3
OUT_ACC = ACC_FIRST + (GROUPS - 2) * ACC_PER_GROUP + ACC_FINAL
TILES_FIRST = 3 * (TPU - 1)
W_FIRST = TPU * len(ORDER)
W_OUT = W_FIRST + (3 * (GROUPS - 2) + 2) * TPU
OUT_TILES = TILES_FIRST + (3 * (GROUPS - 2) + 2) * (TPU - 1)
STORES = [(n * D // 4, (n + 1) * D // 4) for n in range(4)]
Y_AT = [(0, 1, 2), (), (3,), (4, 5), (6,), (), (), ()]
MASK_STEPS = 14


def build(nc, x, c, w_ada, b_ada, g_norm, w_in, g_sb, g_dil, w_out, g_final, out):
    x_rows = x.rearrange("o (s p) d -> p (o s) d", p=P)
    out_rows = out.rearrange("o (s p) d -> p (o s) d", p=P)
    ada_rows = w_ada.rearrange("l (k p) e -> (l k) p e", p=P)
    ada_tiles = w_ada.rearrange("l (t k p) e -> (l t) p k e", p=P, k=TK)
    in_tiles = w_in.rearrange("l (t k p) e -> (l t) p k e", p=P, k=TK)
    out_tiles = w_out.rearrange("l (t k p) e -> (l t) p k e", p=P, k=TK)

    with ExitStack() as ctx:
        def sb(name, shape, dt=F32):
            return ctx.enter_context(nc.sbuf_tensor(name, shape, dt))

        def sem(name):
            return ctx.enter_context(nc.semaphore(name))

        act_split = sb("act_split", [P, KC, 2 * S], F32R)
        act_t = sb("act_t", [P, KC, S])
        xnew = act_t[:, :, :].rearrange("p k s -> p (k s)").rearrange("p (s d) -> p s d", s=SB)
        ring = sb("ring", [P, RING, TILE])
        w_hi = sb("w_hi", [P, 2, TK, GW], F32R)
        w_lo = sb("w_lo", [P, 2, TK, GW], F32R)
        ada_acc = sb("ada_acc", [P, D])
        mod_acc = ada_acc[:, :].rearrange("p (j kk a e) -> p j kk a e", j=2, kk=2, a=2)
        heads_in = sb("heads_in", [P, 4, HG * S])
        q_t = heads_in[:, 0, :].rearrange("p (j s) -> p j s", j=HG)
        k_t = heads_in[:, 1, :].rearrange("p (j s) -> p j s", j=HG)
        k_final = heads_in[:, 2, :].rearrange("p (j s) -> p j s", j=HG)
        squares = heads_in[:, 2, :].rearrange("p (s e) -> p s e", s=SB)
        y_nat = heads_in[:, 3, :].rearrange("p (j s d) -> p j s d", j=HG, s=SB)
        gate_row = heads_in[:, 0, :].rearrange("p (a e) -> p a e", a=2)
        res = heads_in[:, 1, :].rearrange("p (s e) -> p s e", s=SB)
        v_ones = sb("v_ones", [P, SB, HG, VW])
        attn = sb("attn", [P, 2 * HG * KEYS + 2 * KEYS + 2 * (KEYS + 2)])
        probs = attn[:, 0:HG * KEYS].rearrange("p (j c) -> p j c", j=HG)
        probs_t = attn[:, HG * KEYS:2 * HG * KEYS].rearrange("p (j c) -> p j c", j=HG)
        at = 2 * HG * KEYS
        keep = attn[:, at:at + 2 * KEYS].rearrange("p (a c) -> p a c", a=2)
        at += 2 * KEYS
        left = attn[:, at:at + 2 * (KEYS + 2)].rearrange("p (a c) -> p a c", a=2)
        x_half = attn[:, 0:D]
        scratch = act_t[:, :, :].rearrange("p k s -> p (k s)")
        pos_t = scratch[:, 0:KEYS].bitcast(I32)
        pos_n = scratch[:, KEYS:2 * KEYS].bitcast(I32)
        tmp = [scratch[:, (2 + i) * KEYS:(3 + i) * KEYS] for i in range(4)]
        z_set = [act_t[:, u * TK:(u + 1) * TK, :].rearrange("p k s -> p (k s)") for u in range(GROUPS)]
        sum_at = [heads_in[:, 0, :], heads_in[:, 1, :], heads_in[:, 3, :]] + [
            attn[:, n * HG * S:(n + 1) * HG * S] for n in range(4)] + [z_set[0], heads_in[:, 2, :]]
        whole_at = [z_set[G] for _, G in SUMMED[:NZ]] + [heads_in[:, 2, :]]
        sigma_at = sum_at[:NZ - 1] + [heads_in[:, 3, :]]
        part = v_ones
        g_final_row = sb("g_final_row", [P, GW])
        ident = sb("ident", [P, P])
        diag = sb("diag", [P, P])
        ones = sb("ones", [P, P])
        stop_mask = sb("stop_mask", [P, KEYS], BF16)
        dist_mask = sb("dist_mask", [P, KEYS], BF16)
        causal_t = sb("causal_t", [P, KEYS], BF16)
        count_t = sb("count_t", [P, KEYS], BF16)
        vec_rows = sb("vec_rows", [3 * KC, P])
        vec_t = sb("vec_t", [P, 3 * KC])
        bias_rows = sb("bias_rows", [2 * KC, P])
        bias_t = sb("bias_t", [P, PHASES, 2, TK])
        c_t = sb("c_t", [P, KC])
        mod_t = sb("mod_t", [P, 2, TK])
        mul_t = sb("mul_t", [P, TK])
        slope = sb("slope", [P, len(SLOPES)])
        neg_max = sb("neg_max", [P, HG, SB])
        sums = sb("sums", [P, HG, SB])
        dens = sb("dens", [P, HG, SB])
        den_sq = sb("den_sq", [P, HG, SB])
        rstd = sb("rstd", [P, HG, SB])
        minus_half = sb("minus_half", [P, HG, SB])
        x_sum = sb("x_sum", [P, SB])
        out_sums = sb("out_sums", [P, SB, OUT_UNITS])
        out_sum = sb("out_sum", [P, SB])
        out_rstd = sb("out_rstd", [P, SB])

        acc = ctx.enter_context(nc.psum_tensor("acc", [P, 4, 512], F32))
        att = ctx.enter_context(nc.psum_tensor("att", [P, 4, 512], F32))

        raw_ready = [sem(f"raw_ready{i}") for i in range(RING)]
        ring_used = sem("ring_used")
        hi_ready = sem("hi_ready")
        tile_done = sem("tile_done")
        part_done = sem("part_done")
        part_taken = sem("part_taken")
        part_summed = sem("part_summed")
        sigma_ready = sem("sigma_ready")
        z_ready = sem("z_ready")
        acc_done = sem("acc_done")
        cross_ready = sem("cross_ready")
        acc_taken = sem("acc_taken")
        vec_ready = sem("vec_ready")
        gate_seeded = sem("gate_seeded")
        x_ready = sem("x_ready")
        ident_ready = sem("ident_ready")
        zeroed = sem("zeroed")
        pos_ready = sem("pos_ready")
        mask_step = sem("mask_step")
        vec_turned = sem("vec_turned")
        vec_copied = sem("vec_copied")
        c_sigma = sem("c_sigma")
        c_ready = sem("c_ready")
        x_squared = sem("x_squared")
        x_stat = sem("x_stat")
        x_turned = sem("x_turned")
        x_copied = sem("x_copied")
        mod_part = sem("mod_part")
        mod_summed = sem("mod_summed")
        mod_ready = sem("mod_ready")
        h_ready = sem("h_ready")
        split_hi = sem("split_hi")
        split_lo = sem("split_lo")
        ones_set = sem("ones_set")
        scores_ready = sem("scores_ready")
        keep_ready = sem("keep_ready")
        left_ready = sem("left_ready")
        probs_a = sem("probs_a")
        biased = sem("biased")
        max_ready = sem("max_ready")
        probs_b = sem("probs_b")
        probs_turned = sem("probs_turned")
        probs_t_ready = sem("probs_t_ready")
        y_ready = sem("y_ready")
        y_squared = sem("y_squared")
        den_step = sem("den_step")
        var_ready = sem("var_ready")
        rstd_ready = sem("rstd_ready")
        y_normed = sem("y_normed")
        y_turned = sem("y_turned")
        y_taken = sem("y_taken")
        gate_ready = sem("gate_ready")
        gate_copied = sem("gate_copied")
        xg_ready = sem("xg_ready")
        res_ready = sem("res_ready")
        gained = sem("gained")
        res_squared = sem("res_squared")
        tail_step = sem("tail_step")
        out_rstd_ready = sem("out_rstd_ready")
        scaled = [sem("scaled_first"), sem("scaled_second")]
        out_done = sem("out_done")

        def acc_before(g, t):
            return g * ACC_PER_GROUP + ACC_AT[t] + ACC_FIRST - ACC_PER_GROUP

        def unit_entry(kind, t):
            return sum(TPU + len(GATES[kind][u]) for u in range(t))

        def weight_entry(kind, t, i):
            return unit_entry(kind, t) + [e for e in range(2 * TPU) if e not in GATES[kind][t]][i]

        def landed(n):
            return 16 * (n // RING + 1)

        def phase_wait(eng, j, e):
            per = PHASE_ENTRIES // RING
            eng.wait_ge(raw_ready[e % RING], j * (16 * per) + landed(FIRST_ENTRIES + e) - 16 * per)

        def last_wait(eng, e):
            eng.wait_ge(raw_ready[e % RING], landed(LAST_BASE + e))

        def entry_wait(eng, g, kind, n):
            eng.wait_ge(raw_ready[n % RING], g * (16 * ENTRIES[kind] // RING) + landed(GROUP_BASE[kind] + n))

        def out_entry_wait(eng, v, e):
            eng.wait_ge(raw_ready[e % RING], v * (16 * TPU // RING) + landed(OUT_BASE + e))

        def positions(what, entries):
            return [e for e, k in enumerate(entries) if k == what]

        block = ctx.enter_context(nc.Block())

        @block.sync
        def _(sp):
            def tile(slot, src):
                sp.dma_start(ring[:, slot, :].rearrange("p (k e) -> p k e", k=TK), src).then_inc(raw_ready[slot], 16)

            def gate(slot, k, half):
                lo = 2 * D + half * (D // 2)
                sp.dma_start(ring[:, slot, :], ada_rows[k, :, lo:lo + D // 2]).then_inc(raw_ready[slot], 16)

            def in_col(g_part, g_rest, t):
                return g_part * (PARTS * SB_HEADS * P) + g_rest * GW + t * SB_HEADS * P

            for n in range(ADA_TILES):
                if n >= RING:
                    sp.wait_ge(ring_used, n - RING + 1)
                tile(n % RING, ada_tiles[n // 2, :, :, n % 2 * D:n % 2 * D + GW])
            def order_col(r):
                name, G = ORDER[r]
                return in_col(G // SB_GROUPS, G % SB_GROUPS, "qkvz".index(name))

            with sp.Fori(1, PHASES) as j:
                for e, what in enumerate(PHASE):
                    sp.wait_ge(ring_used, j * PHASE_ENTRIES + FIRST_ENTRIES - PHASE_ENTRIES + e - RING + 1)
                    if what == "a":
                        n = positions("a", PHASE).index(e)
                        tile(e % RING, ada_tiles[n // 2, :, :, bass.ds(j * GW + n % 2 * D, GW)])
                    else:
                        col = order_col(positions("w", PHASE).index(e))
                        tile(e % RING, in_tiles[j - 1, :, :, col:col + GW])
            for e, what in enumerate(LAST):
                sp.wait_ge(ring_used, LAST_BASE + e - RING + 1)
                if what == "w":
                    col = order_col(positions("w", LAST).index(e))
                    tile(e % RING, in_tiles[TPU - 1, :, :, col:col + GW])
                else:
                    n = positions("g", LAST).index(e)
                    gate(e % RING, n // 2, n % 2)

            def group(g, kind, part, rest):
                ng = 0
                for t, name in enumerate(UNITS[kind]):
                    i = 0
                    for e in range(TPU + len(GATES[kind][t])):
                        n = unit_entry(kind, t) + e
                        sp.wait_ge(ring_used, g * ENTRIES[kind] + GROUP_BASE[kind] + n - RING + 1)
                        if e in GATES[kind][t]:
                            gate(n % RING, g * GATE_CHUNKS[kind] + GATE_BASE[kind] + ng // 2, ng % 2)
                            ng += 1
                        else:
                            tile(n % RING, in_tiles[i, :, :, bass.ds(in_col(part, rest, "qkvz".index(name)), GW)])
                            i += 1

            with sp.Fori(1, SB_GROUPS) as g:
                group(g, "wide", 0, g)
            group(SB_GROUPS, "wide", 1, 0)
            with sp.Fori(WIDE_GROUPS, GROUPS - 1) as g:
                group(g, "narrow", 1, g - SB_GROUPS)
            group(GROUPS - 1, "final", 1, GROUPS - 1 - SB_GROUPS)

            def out_piece(v):
                sp.dma_start(g_final_row[:, :], g_final[bass.ds(v * GW, GW)].rearrange("(o e) -> o e", o=1)
                             .to_broadcast([P, GW])).then_inc(xg_ready, 16)
                sp.wait_ge(split_lo, 2 * TPU)
                sp.dma_start(xnew[:, :, bass.ds(v * GW, GW)], x_rows[:, :, bass.ds(v * GW, GW)]).then_inc(xg_ready, 16)

            def out_unit(v, first=False):
                for e in range(TPU):
                    sp.wait_ge(ring_used, v * TPU + OUT_BASE + e - RING + 1)
                    sp.dma_start(ring[:, e % RING, :].rearrange("p (k e) -> p k e", k=TK),
                                 out_tiles[e, :, :, bass.ds(v * GW, GW)]).then_inc(raw_ready[e % RING], 16)
                    if e == 0 and not first:
                        if not isinstance(v, int) or v > 1:
                            sp.wait_ge(gained, v * SB - SB)
                        out_piece(v - 1)

            out_unit(0, first=True)
            out_unit(1)
            with sp.Fori(1, OUT_UNITS // 2) as i:
                out_unit(i * 2)
                out_unit(i * 2 + 1)
            sp.wait_ge(gained, (OUT_UNITS - 1) * SB)
            out_piece(OUT_UNITS - 1)
            for s in range(SB):
                for n, (lo, hi) in enumerate(STORES):
                    sp.wait_ge(scaled[s], n + 1)
                    sp.dma_start(out_rows[:, s, lo:hi], xnew[:, s, lo:hi]).then_inc(out_done, 16)
            sp.wait_ge(out_done, 2 * 16 * len(STORES))

        @block.gpsimd
        def _(pool):
            pool.memset(ident[:, :], 0.0).then_inc(ident_ready, 1)
            pool.wait_ge(ident_ready, 1)
            pool.affine_select(out=ident[:, :], in_=ident[:, :], compare_op=ALU.not_equal, fill=1.0, base=0,
                               pattern=[[-1, P]], channel_multiplier=1).then_inc(ident_ready, 1)
            for a, dq in ((0, 0), (1, P), (2, 0)):
                pool.iota(pos_t[:, a * P:(a + 1) * P], pattern=[[1, P]], base=dq, channel_multiplier=-1)
                pool.iota(pos_n[:, a * P:(a + 1) * P], pattern=[[-1, P]], base=dq, channel_multiplier=1).then_inc(pos_ready, 1)
            pool.memset(ones[:, :], 1.0)
            for h, s in enumerate(SLOPES):
                pool.memset(slope[:, h:h + 1], s)
            pool.memset(minus_half[:, :, :], -0.5).then_inc(ident_ready, 1)
            pool.wait_ge(ident_ready, 3)
            for s in range(SB):
                pool.wait_ge(x_squared, s + 1)
                pool.tensor_scalar(x_sum[:, s:s + 1], x_sum[:, s:s + 1], 1.0 / D, EPS, ALU.mult, ALU.add).then_inc(x_stat, 1)
                pool.wait_ge(x_stat, 3 * s + 1)
                pool.tensor_tensor(x_sum[:, s:s + 1], x_sum[:, s:s + 1], minus_half[:, 0, 0:1], ALU.pow).then_inc(x_stat, 1)
                pool.wait_ge(x_stat, 3 * s + 2)
                if s:
                    pool.wait_ge(x_turned, TPU)
                pool.tensor_scalar(diag[:, :], ident[:, :], x_sum[:, s:s + 1], None, ALU.mult).then_inc(x_stat, 1)

            def act_lo(i, n):
                pool.wait_ge(split_hi, n + 1)
                pool.tensor_tensor(act_split[:, bass.ds(i * TK, TK), S:2 * S], act_t[:, bass.ds(i * TK, TK), :],
                                   act_split[:, bass.ds(i * TK, TK), 0:S].bitcast(F32), ALU.subtract).then_inc(split_lo, 1)

            pool.wait_ge(x_turned, 2 * TPU)
            pool.memset(v_ones[:, :, :, P:VW], 1.0)

            def adds(j, u):
                for s in range(SB):
                    n = (u - NS) * SB + s + 1
                    pool.wait_ge(part_taken, j * (NS * SB) + n)
                    share = part[:, s, :, 0:P]
                    total = sum_at[u][:, s * GW:(s + 1) * GW].rearrange("p (j e) -> p j e", j=HG)
                    if isinstance(j, int) and j == 1:
                        pool.tensor_copy(total, share).then_inc(part_summed, 1)
                        continue
                    dst = total
                    if isinstance(j, int) and j == PHASES:
                        dst = whole_at[u][:, s * GW:(s + 1) * GW].rearrange("p (j e) -> p j e", j=HG)
                    pool.wait_ge(part_summed, (j - 1) * (NS * SB) + n)
                    pool.tensor_tensor(dst, share, total, ALU.add).then_inc(part_summed, 1)

            def z_silu(u):
                pool.wait_ge(sigma_ready, u + 1)
                pool.tensor_tensor(whole_at[u], whole_at[u], sigma_at[u], ALU.mult).then_inc(z_ready, 1)

            act_lo(0, 0)
            pool.wait_ge(split_lo, 1)
            for u in range(NS):
                adds(1, u)
            with pool.Fori(2, PHASES) as j:
                act_lo(j - 1, j - 1)
                for u in range(NS):
                    adds(j, u)
            act_lo(PHASES - 1, PHASES - 1)
            pool.wait_ge(mod_summed, PHASES)
            pool.memset(ada_acc[:, :], 0.0).then_inc(zeroed, 1)
            for u in range(NS):
                adds(PHASES, u)
                if u:
                    z_silu(u - 1)
            pool.wait_ge(z_ready, NZ)
            pool.memset(left[:, :, P:P + 1], 1.0)
            pool.memset(left[:, :, KEYS + 1:KEYS + 2], 1.0).then_inc(ones_set, 1)

            def group_rstd(g):
                pool.wait_ge(var_ready, g + 1)
                pool.tensor_tensor(rstd[:, :, :], sums[:, :, :], minus_half[:, :, :], ALU.pow).then_inc(rstd_ready, 1)

            with pool.Fori(0, GROUPS - 1) as g:
                group_rstd(g)
            for i in range(TPU - 2):
                act_lo(i, TPU + i)
            group_rstd(GROUPS - 1)
            act_lo(TPU - 2, 2 * TPU - 2)
            for s in range(SB):
                pool.wait_ge(tail_step, 2 * s + 2)
                pool.tensor_tensor(out_rstd[:, s:s + 1], out_sum[:, s:s + 1], minus_half[:, 0, 0:1], ALU.pow).then_inc(out_rstd_ready, 1)

        @block.scalar
        def _(act):
            act.dma_start(vec_rows[0:KC, :], c.rearrange("o (k p) -> (o k) p", p=P)).then_inc(vec_ready, 16)
            act.dma_start(vec_rows[KC:2 * KC, :], g_norm.rearrange("l (k p) -> (l k) p", p=P)).then_inc(vec_ready, 16)
            act.dma_start(vec_rows[2 * KC:2 * KC + SB_HEADS, :], g_sb.rearrange("l (k p) -> (l k) p", p=P)).then_inc(vec_ready, 16)
            act.dma_start(vec_rows[2 * KC + SB_HEADS:3 * KC, :], g_dil.rearrange("l (k p) -> (l k) p", p=P)).then_inc(vec_ready, 16)
            act.dma_start(bias_rows[0:KC, :], b_ada[:, 0:D].rearrange("l (k p) -> (l k) p", p=P)).then_inc(vec_ready, 16)
            act.dma_start(bias_rows[KC:2 * KC, :], b_ada[:, D:2 * D].rearrange("l (k p) -> (l k) p", p=P)).then_inc(vec_ready, 16)
            act.dma_start(x_half, x_rows[:, 0, :]).then_inc(x_ready, 16)
            act.wait_ge(vec_copied, 1)
            act.activation(c_t[:, :], vec_t[:, 0:KC], ACT.Sigmoid).then_inc(c_sigma, 1)
            act.wait_ge(mask_step, MASK_STEPS)
            for s in range(SB):
                act.wait_ge(x_ready, 16 * (s + 1))
                act.activation(act_t[:, :, s * P:(s + 1) * P], x_half.rearrange("p (k e) -> p k e", k=KC), ACT.Square,
                               accum_out=x_sum[:, s:s + 1]).then_inc(x_squared, 1)
                act.wait_ge(x_squared, s + 1)
                for b in range(TPU):
                    act.wait_ge(x_turned, s * TPU + b + 1)
                    act.activation(act_t[:, b * TK:(b + 1) * TK, s * P:(s + 1) * P],
                                   acc[:, b % 4, :].rearrange("p (k e) -> p k e", k=TK), ACT.Copy).then_inc(x_copied, 1)
                if s == 0:
                    act.dma_start(x_half, x_rows[:, 1, :]).then_inc(x_ready, 16)

            def hi(slot, m, m1):
                act.activation(w_hi[:, m1, :, :].rearrange("p k e -> p (k e)"), ring[:, slot, :], ACT.Copy).then_inc(hi_ready, 1)

            def split(g, kind, t, i):
                done = g * (3 * (TPU - 1)) + TILES_FIRST - 3 * (TPU - 1) + t * (TPU - 1)
                if i >= 2:
                    act.wait_ge(tile_done, done + i - 1)
                elif i == 0:
                    act.wait_ge(tile_done, done)
                else:
                    act.wait_ge(acc_done, acc_before(g, t))
                n = weight_entry(kind, t, i) if t < len(UNITS[kind]) else ENTRIES[kind]
                entry_wait(act, g, kind, n)
                hi(n % RING, i, i % 2)

            def out_split(v, i):
                if i >= 2:
                    act.wait_ge(tile_done, v * (TPU - 1) + OUT_TILES + i - 1)
                elif i == 0:
                    act.wait_ge(tile_done, v * (TPU - 1) + OUT_TILES)
                else:
                    act.wait_ge(acc_done, v * SB + OUT_ACC)
                out_entry_wait(act, v, i)
                hi(i % RING, i, i % 2)

            def take(g, t, name):
                if name in "qk":
                    dst, scale = {"q": (q_t, INV_SQRT_D), "k": (k_t, 1.0)}[name]
                    for j in range(HG):
                        act.wait_ge(acc_done, acc_before(g, t) + j + 1)
                        act.activation(dst[:, j, :], acc[:, j, S:2 * S], ACT.Copy,
                                       scale=scale).then_inc(cross_ready, 1)

            def h_hi(j):
                act.wait_ge(h_ready, j + 1)
                act.activation(act_split[:, bass.ds(j * TK, TK), 0:S], act_t[:, bass.ds(j * TK, TK), :], ACT.Copy).then_inc(split_hi, 1)

            def y_hi(i):
                if i == 0:
                    act.wait_ge(acc_done, OUT_ACC)
                act.wait_ge(y_taken, HG * (i + 1))
                act.activation(act_split[:, i * TK:(i + 1) * TK, 0:S], act_t[:, i * TK:(i + 1) * TK, :], ACT.Copy).then_inc(split_hi, 1)

            def probs_job(G, stick, j):
                act.wait_ge(scores_ready, G * HG + j + 1) if stick else None
                if stick:
                    if j >= 2:
                        act.wait_ge(probs_a, G * HG + j - 1)
                    act.activation(keep[:, j % 2, :], att[:, j, 0:KEYS], ACT.Sigmoid, scale=-1.0)
                    act.activation(probs[:, j, :], att[:, j, 0:KEYS], ACT.Sigmoid).then_inc(keep_ready, 1)
                else:
                    act.wait_ge(max_ready, G * HG - SB_HEADS + j + 1)
                    act.activation(probs[:, j, 0:P], probs[:, j, 0:P], ACT.Exp, bias=neg_max[:, j, 0:1])
                    act.activation(probs[:, j, P:KEYS], probs[:, j, P:KEYS], ACT.Exp, bias=neg_max[:, j, 1:2]).then_inc(probs_b, 1)

            def square_job(G, j):
                act.wait_ge(y_ready, G * HG + j + 1)
                for s in range(SB):
                    ins = act.activation(y_nat[:, j, s, :], att[:, j, s * VW:s * VW + P], ACT.Square,
                                         accum_out=sums[:, j, s:s + 1])
                ins.then_inc(y_squared, 1)

            def y_job(G, j):
                act.wait_ge(y_turned, G * HG + j // 2 * 2 + 2)
                act.activation(act_t[:, bass.ds(G * HG + j, 1), :].rearrange("p o s -> p (o s)"),
                               att[:, j // 2, (j % 2) * S:(j % 2 + 1) * S], ACT.Copy,
                               scale=vec_t[:, bass.ds(G * HG + j + 2 * KC, 1)]).then_inc(y_taken, 1)

            def job(G, stick, t, n):
                if t == 0 and stick and n < HG:
                    probs_job(G, stick, n)
                elif t == 0 and not stick and 1 <= n < HG + 1:
                    probs_job(G, stick, n - 1)
                elif t == 2 and n < 2:
                    square_job(G, 2 * n)
                    square_job(G, 2 * n + 1)
                elif t == 2 and n == TPU - 2:
                    for h in range(HG):
                        y_job(G, h)

            def multiplied(j, r):
                if U0 <= r < U0 + NS:
                    act.wait_ge(part_done, j * (NS * SB) + (r - U0 + 1 - NS) * SB)
                    return
                n = r + 1 if r < U0 else r - NS + 1
                if isinstance(j, int) and j == PHASES:
                    act.wait_ge(acc_done, 2 * n)
                else:
                    act.wait_ge(tile_done, j * 3 + n - 3)

            def part_take(j, u, s):
                n = (u - NS) * SB + s + 1
                act.wait_ge(part_done, j * (NS * SB) + n)
                if not isinstance(j, int) or j > 1 or u:
                    act.wait_ge(part_summed, j * (NS * SB) + n - SB)
                act.activation(part[:, s, :, 0:P], att[:, 2 + s, :].rearrange("p (j e) -> p j e", j=HG),
                               ACT.Copy).then_inc(part_taken, 1)

            def z_sigma(u):
                act.wait_ge(part_summed, (NS * (PHASES - 1) + u + 1) * SB)
                if u == NZ - 1:
                    act.wait_ge(z_ready, 3)
                act.activation(sigma_at[u], whole_at[u], ACT.Sigmoid).then_inc(sigma_ready, 1)

            def phase(j):
                last = isinstance(j, int) and j == PHASES
                h_hi(j - 1)
                for r in range(len(ORDER)):
                    u = r - 2 - U0
                    if 0 <= u < NS:
                        part_take(j, u, 0)
                    if r >= 2:
                        multiplied(j, r - 2)
                    elif not isinstance(j, int) or j > 1:
                        multiplied(j - 1, len(ORDER) + r - 2)
                    if last:
                        e = positions("w", LAST)[r]
                        last_wait(act, e)
                    else:
                        e = positions("w", PHASE)[r]
                        phase_wait(act, j, e)
                    hi(e % RING, r, r % 2)
                    if 0 <= u < NS:
                        part_take(j, u, 1)
                    if last and r == 2:
                        act.wait_ge(zeroed, 1)
                        act.dma_start(ada_acc[0:1, :], b_ada[:, 2 * D:3 * D]).then_inc(gate_seeded, 16)
                    if last and 1 <= u <= NZ:
                        z_sigma(u - 1)

            phase(1)
            with act.Fori(2, PHASES) as j:
                phase(j)
            phase(PHASES)
            act.wait_ge(acc_done, 4)
            act.wait_ge(raw_ready[0], landed(PROJ_BASE))
            hi(0, 0, 0)
            act.wait_ge(ones_set, 1)

            def group(g, kind, stick):
                G, units = g - 1, UNITS[kind]
                for t in range(len(units)):
                    for i in range(TPU):
                        if t or i:
                            split(g, kind, t, i)
                        if t and i == 0:
                            take(g, t - 1, units[t - 1])
                        if i >= 1:
                            job(G, stick, 2 if t == len(units) - 1 else t, i - 1)
                split(g, kind, len(units), 0)

            with act.Fori(1, WIDE_GROUPS) as g:
                group(g, "wide", True)
            with act.Fori(WIDE_GROUPS, GROUPS - 1) as g:
                group(g, "narrow", False)
            group(GROUPS - 1, "final", False)

            G = GROUPS - 1
            for i in range(TPU):
                if i:
                    out_split(0, i)
                if i in (1, 2):
                    probs_job(G, False, 2 * i - 2)
                    probs_job(G, False, 2 * i - 1)
                for n in Y_AT[i]:
                    y_hi(n)
                if i == 5:
                    for j in range(HG):
                        square_job(G, j)
            for j in range(HG):
                y_job(G, j)
            y_hi(TPU - 1)

            def gate_copy(v, par):
                act.wait_ge(gate_ready, v + 1)
                act.wait_ge(acc_taken, v * SB + OUT_ACC - SB)
                act.activation(gate_row[:, par, :], att[:, 2 + par, :], ACT.Copy).then_inc(gate_copied, 1)

            def square_res(v, halves=range(SB)):
                for s in halves:
                    act.wait_ge(res_ready, v * SB + s + 1)
                    act.activation(squares[:, s, :], res[:, s, :], ACT.Square,
                                   accum_out=out_sums[:, s, bass.ds(v, 1)]).then_inc(res_squared, 1)

            def out_unit(v, par):
                for i in range(TPU):
                    out_split(v, i)
                    if i == 0:
                        gate_copy(v - 1, 1 - par)
                    if i == 3:
                        square_res(v - 1)

            out_unit(1, 1)
            with act.Fori(1, OUT_UNITS // 2) as i:
                out_unit(i * 2, 0)
                out_unit(i * 2 + 1, 1)
            gate_copy(OUT_UNITS - 1, 1)
            square_res(OUT_UNITS - 1, [0])
            act.wait_ge(out_rstd_ready, 1)
            act.wait_ge(gained, (OUT_UNITS - 1) * SB + 1)
            for n, (lo, hi) in enumerate(STORES):
                if n == 1:
                    square_res(OUT_UNITS - 1, [1])
                act.activation(xnew[:, 0, lo:hi], xnew[:, 0, lo:hi], ACT.Copy, scale=out_rstd[:, 0:1]).then_inc(scaled[0], 1)

        @block.vector
        def _(dve):
            dve.wait_ge(pos_ready, 3)
            steps = [0]

            def step(ins):
                ins.then_inc(mask_step, 1)
                steps[0] += 1
                dve.wait_ge(mask_step, steps[0])

            low4, low16 = tmp[0].bitcast(I32), tmp[1].bitcast(I32)
            f0, f1 = tmp[2], tmp[3]
            step(dve.tensor_scalar(low4, pos_t, 3, None, ALU.bitwise_and))
            step(dve.tensor_scalar(low16, pos_t, 15, None, ALU.bitwise_and))
            step(dve.tensor_scalar(f0, low4, 0.0, None, ALU.is_equal))
            step(dve.scalar_tensor_tensor(f1, low16, 0.0, f0, ALU.is_equal, ALU.add))
            step(dve.scalar_tensor_tensor(f0, pos_t, float(WINDOW), f1, ALU.is_le, ALU.add))
            step(dve.scalar_tensor_tensor(count_t[:, :], pos_t, 0.0, f0, ALU.is_ge, ALU.mult))
            step(dve.tensor_scalar(causal_t[:, :], pos_t, 0.0, None, ALU.is_gt))
            step(dve.tensor_scalar(stop_mask[:, :], pos_n, 0.0, None, ALU.is_le))
            step(dve.tensor_scalar(low4, pos_n, 3, None, ALU.bitwise_and))
            step(dve.tensor_scalar(f0, low4, 0.0, None, ALU.is_equal))
            step(dve.scalar_tensor_tensor(f1, pos_n, float(WINDOW), f0, ALU.is_le, ALU.max))
            step(dve.scalar_tensor_tensor(f0, pos_n, 0.0, f1, ALU.is_ge, ALU.mult))
            step(dve.tensor_scalar(f1, f0, -MASKED, MASKED, ALU.mult, ALU.add))
            step(dve.tensor_tensor(dist_mask[:, :], f1, pos_n, ALU.subtract))

            assert steps[0] == MASK_STEPS

            dve.wait_ge(vec_turned, 1)
            for a in range(2):
                dve.tensor_copy(bias_t[:, :, a, :], att[:, 1, a * KC:(a + 1) * KC].rearrange("p (j k) -> p j k", k=TK))
            dve.tensor_copy(vec_t[:, :], att[:, 0, 0:3 * KC]).then_inc(vec_copied, 1)
            dve.wait_ge(c_sigma, 1)
            dve.wait_ge(vec_copied, 1)
            dve.tensor_tensor(c_t[:, :], c_t[:, :], vec_t[:, 0:KC], ALU.mult).then_inc(c_ready, 1)
            dve.wait_ge(c_ready, 1)

            def ada(slot, j, par, n):
                for kk in range(TK):
                    cols = mod_acc[:, par, kk % 2, n % 2, :]
                    w = ring[:, slot, kk * GW:(kk + 1) * GW]
                    k = n // 2 * TK + kk
                    if kk >= 2:
                        dve.wait_ge(mod_part, j * (2 * ADA_TILES) + 2 * n + kk - 1)
                    if n < 2 and kk < 2:
                        ins = dve.tensor_scalar(cols, w, c_t[:, k:k + 1], None, ALU.mult)
                    else:
                        ins = dve.scalar_tensor_tensor(cols, w, c_t[:, k:k + 1], cols, ALU.mult, ALU.add)
                    if kk < 2:
                        ins.then_inc(mod_part, 1)
                ins.then_inc(ring_used, 1)

            def lo(slot, par):
                dve.tensor_tensor(w_lo[:, par, :, :].rearrange("p k e -> p (k e)"), ring[:, slot, :],
                                  w_hi[:, par, :, :].rearrange("p k e -> p (k e)").bitcast(F32), ALU.subtract).then_inc(ring_used, 1)

            def modulate(j):
                dve.wait_ge(mod_summed, j + 1)
                dve.tensor_tensor(mod_t[:, :, :], att[:, 3, 0:2 * TK].rearrange("p (a k) -> p a k", a=2),
                                  bias_t[:, bass.ds(j, 1), :, :].rearrange("p o a k -> p (o a) k"), ALU.add).then_inc(mod_ready, 1)
                dve.wait_ge(mod_ready, j * 2 + 1)
                dve.scalar_tensor_tensor(mul_t[:, :], mod_t[:, 1, :], 1.0, vec_t[:, bass.ds(j * TK + KC, TK)],
                                         ALU.add, ALU.mult).then_inc(mod_ready, 1)
                dve.wait_ge(mod_ready, j * 2 + 2)
                for k in range(TK):
                    chunk = act_t[:, bass.ds(j * TK + k, 1), :].rearrange("p o s -> p (o s)")
                    ins = dve.tensor_scalar(chunk, chunk, mul_t[:, k:k + 1], mod_t[:, 0, k:k + 1], ALU.mult, ALU.add)
                ins.then_inc(h_ready, 1)

            def split(g, kind, t, i):
                dve.wait_ge(hi_ready, g * (3 * TPU) + W_FIRST - 3 * TPU + t * TPU + i + 1)
                n = weight_entry(kind, t, i) if t < len(UNITS[kind]) else ENTRIES[kind]
                lo(n % RING, i % 2)

            for n in range(ADA_TILES):
                dve.wait_ge(raw_ready[n % RING], 16 * (n // RING + 1))
                if n >= 2:
                    dve.wait_ge(ring_used, n - 1)
                ada(n % RING, 0, 0, n)
            dve.wait_ge(x_copied, 2 * TPU)

            def phase(j, par):
                n = r = 0
                for e, what in enumerate(PHASE):
                    if what == "a":
                        phase_wait(dve, j, e)
                        if n >= 2:
                            dve.wait_ge(ring_used, j * PHASE_ENTRIES + FIRST_ENTRIES - PHASE_ENTRIES + e - 1)
                        ada(e % RING, j, par, n)
                        n += 1
                        if n == 4:
                            modulate(j - 1)
                    else:
                        dve.wait_ge(hi_ready, j * len(ORDER) + r + 1 - len(ORDER))
                        lo(e % RING, r % 2)
                        r += 1

            with dve.Fori(0, (PHASES - 1) // 2) as i:
                phase(i * 2 + 1, 1)
                phase(i * 2 + 2, 0)
            phase(PHASES - 1, 1)
            modulate(PHASES - 1)

            def gate_tile(slot, k, half):
                cols = ada_acc[:, half * (D // 2):(half + 1) * (D // 2)]
                dve.scalar_tensor_tensor(cols, ring[:, slot, :], c_t[:, bass.ds(k, 1)], cols, ALU.mult, ALU.add).then_inc(ring_used, 1)

            nw = ng = 0
            for e, what in enumerate(LAST):
                if what == "w":
                    dve.wait_ge(hi_ready, (PHASES - 1) * len(ORDER) + nw + 1)
                    lo(e % RING, nw % 2)
                    nw += 1
                else:
                    if ng == 0:
                        dve.wait_ge(gate_seeded, 16)
                    if ng >= 2:
                        dve.wait_ge(ring_used, LAST_BASE + e - 1)
                    last_wait(dve, e)
                    gate_tile(e % RING, ng // 2, ng % 2)
                    ng += 1
            dve.wait_ge(z_ready, 2)
            dve.wait_ge(acc_done, 2)
            for b in range(2):
                dve.tensor_scalar(q_t[:, 2 * b:2 * b + 2, :].rearrange("p j s -> p (j s)"), acc[:, b, :], INV_SQRT_D, None,
                                  ALU.mult).then_inc(acc_taken, 1)
            dve.wait_ge(acc_done, 4)
            for b in range(2):
                dve.tensor_copy(k_t[:, 2 * b:2 * b + 2, :].rearrange("p j s -> p (j s)"), acc[:, 2 + b, :]).then_inc(acc_taken, 1)
            dve.wait_ge(hi_ready, W_FIRST + 1)
            lo(0, 0)
            dve.wait_ge(ones_set, 1)
            for s in range(SB):
                dve.wait_ge(acc_done, 4 + s + 1)
                dve.tensor_copy(v_ones[:, s, :, 0:P], att[:, s, :].rearrange("p (j e) -> p j e", j=HG)).then_inc(acc_taken, 1)

            def out_split(v, i):
                dve.wait_ge(hi_ready, v * TPU + W_OUT + i + 1)
                lo(i % RING, i % 2)

            def gate(g, kind, t, m):
                n = unit_entry(kind, t) + GATES[kind][t][m]
                i = sum(len(GATES[kind][u]) for u in range(t)) + m
                entry_wait(dve, g, kind, n)
                gate_tile(n % RING, g * GATE_CHUNKS[kind] + GATE_BASE[kind] + i // 2, i % 2)

            def take(g, t, name):
                if name in "qk":
                    dst = {"q": q_t, "k": k_t}[name]
                    for j in range(HG):
                        dve.wait_ge(cross_ready, g * (2 * HG) + t * HG + j + 1 - 2 * HG)
                        if name == "q":
                            dve.scalar_tensor_tensor(dst[:, j, :], acc[:, j, 0:S], INV_SQRT_D, dst[:, j, :],
                                                     ALU.mult, ALU.add).then_inc(acc_taken, 1)
                        else:
                            dve.tensor_tensor(dst[:, j, :], acc[:, j, 0:S], dst[:, j, :], ALU.add).then_inc(acc_taken, 1)
                else:
                    for s in range(SB):
                        dve.wait_ge(acc_done, acc_before(g, t) + s + 1)
                        dve.tensor_copy(v_ones[:, s, :, 0:P], acc[:, s, :].rearrange("p (j e) -> p j e", j=HG)).then_inc(acc_taken, 1)

            def probs_job(G, stick, j):
                if stick:
                    dve.wait_ge(keep_ready, G * HG + j + 1)
                    dve.tensor_tensor_scan(left[:, j % 2, 0:P][:, ::-1], keep[:, j % 2, 0:P][:, ::-1],
                                           stop_mask[:, 0:P][:, ::-1], 1.0, ALU.mult, ALU.max)
                    dve.tensor_tensor_scan(left[:, j % 2, P + 1:KEYS + 1][:, ::-1], keep[:, j % 2, P:KEYS][:, ::-1],
                                           stop_mask[:, P:KEYS][:, ::-1], 1.0, ALU.mult, ALU.max).then_inc(left_ready, 1)
                    dve.wait_ge(left_ready, G * HG + j + 1)
                    dve.tensor_tensor(probs[:, j, 0:P], probs[:, j, 0:P], left[:, j % 2, 1:P + 1], ALU.mult)
                    dve.tensor_tensor(probs[:, j, P:KEYS], probs[:, j, P:KEYS], left[:, j % 2, P + 2:KEYS + 2],
                                      ALU.mult).then_inc(probs_a, 1)
                else:
                    n = G * HG - SB_HEADS + j
                    dve.wait_ge(scores_ready, G * HG + j + 1)
                    dve.scalar_tensor_tensor(probs[:, j, :], dist_mask[:, :], slope[:, bass.ds(n, 1)], att[:, j, 0:KEYS],
                                             ALU.mult, ALU.add).then_inc(biased, 1)
                    dve.wait_ge(biased, n + 1)
                    dve.tensor_reduce(neg_max[:, j, 0:1], probs[:, j, 0:P], AX.X, ALU.max, negate=True)
                    dve.tensor_reduce(neg_max[:, j, 1:2], probs[:, j, P:KEYS], AX.X, ALU.max, negate=True).then_inc(max_ready, 1)

            def turned_job(G, stick, j):
                dve.wait_ge(probs_turned, G * HG + j + 1)
                dve.tensor_tensor(probs_t[:, j, :], att[:, j, 0:KEYS], (causal_t if stick else count_t)[:, :],
                                  ALU.mult).then_inc(probs_t_ready, 1)

            def variance_job(G, stick):
                dve.wait_ge(y_squared, G * HG + HG)
                if stick:
                    dve.tensor_scalar(sums[:, :, :], sums[:, :, :], 1.0 / P, EPS, ALU.mult, ALU.add).then_inc(var_ready, 1)
                    return
                n = G * 2 - 2 * SB_GROUPS
                for s in range(SB):
                    ins = dve.tensor_copy(dens[:, :, s:s + 1], att[:, :, s * VW + P:s * VW + P + 1])
                ins.then_inc(den_step, 1)
                dve.wait_ge(den_step, n + 1)
                dve.scalar_tensor_tensor(den_sq[:, :, :], dens[:, :, :], EPS, dens[:, :, :], ALU.mult, ALU.mult).then_inc(den_step, 1)
                dve.wait_ge(den_step, n + 2)
                dve.scalar_tensor_tensor(sums[:, :, :], sums[:, :, :], 1.0 / P, den_sq[:, :, :], ALU.mult, ALU.add).then_inc(var_ready, 1)

            def norm_job(G, j):
                if j == 0:
                    dve.wait_ge(rstd_ready, G + 1)
                for s in range(SB):
                    at = s * GW + j * P
                    z = act_t[:, bass.ds(G * TK + at // S, 1), at % S:at % S + P].rearrange("p o e -> p (o e)")
                    ins = dve.scalar_tensor_tensor(y_nat[:, j, s, :], att[:, j, s * VW:s * VW + P], rstd[:, j, s:s + 1],
                                                   z, ALU.mult, ALU.mult)
                ins.then_inc(y_normed, 1)

            def job(G, stick, t, n):
                if t == 0 and n < HG:
                    probs_job(G, stick, n)
                elif t == 1 and n < HG:
                    turned_job(G, stick, n)
                elif t == 2 and n == 2:
                    variance_job(G, stick)
                elif t == 2 and n in (3, 4):
                    norm_job(G, 2 * n - 6)
                    norm_job(G, 2 * n - 5)

            def group(g, kind, stick):
                G, units = g - 1, UNITS[kind]
                for t in range(len(units)):
                    m = 0
                    for i in range(TPU):
                        if t or i:
                            split(g, kind, t, i)
                        if t and i == 0:
                            take(g, t - 1, units[t - 1])
                        if i >= 1:
                            job(G, stick, 2 if t == len(units) - 1 else t, i - 1)
                        if kind == "final" and t == 0 and i == TPU - 2:
                            for j in range(HG):
                                turned_job(G, stick, j)
                        while m < len(GATES[kind][t]) and (
                                i == TPU - 1 or weight_entry(kind, t, i + 1) > unit_entry(kind, t) + GATES[kind][t][m]):
                            gate(g, kind, t, m)
                            m += 1
                split(g, kind, len(units), 0)
                take(g, len(units) - 1, "v")

            with dve.Fori(1, WIDE_GROUPS) as g:
                group(g, "wide", True)
            with dve.Fori(WIDE_GROUPS, GROUPS - 1) as g:
                group(g, "narrow", False)
            group(GROUPS - 1, "final", False)

            G = GROUPS - 1
            for i in range(TPU):
                if i:
                    out_split(0, i)
                if i == 1:
                    for j in range(HG):
                        probs_job(G, False, j)
                if i == 3:
                    for j in range(HG):
                        turned_job(G, False, j)
                if i == 5:
                    variance_job(G, False)
                    for j in range(HG):
                        norm_job(G, j)
            dve.wait_ge(split_hi, 2 * TPU)
            dve.wait_ge(split_lo, 2 * TPU - 1)
            k = (TPU - 1) * TK
            dve.tensor_tensor(act_split[:, k:KC, S:2 * S], act_t[:, k:KC, :], act_split[:, k:KC, 0:S].bitcast(F32),
                              ALU.subtract).then_inc(split_lo, 1)

            def finish(v, par):
                dve.wait_ge(gate_copied, v + 1)
                dve.wait_ge(xg_ready, v * 32 + 32)
                if not isinstance(v, int) or v:
                    dve.wait_ge(res_squared, v * SB)
                    dve.wait_ge(gained, v * SB)
                cols = bass.ds(v * GW, GW)
                for s in range(SB):
                    dve.wait_ge(acc_done, v * SB + OUT_ACC + s + 1)
                    dve.tensor_tensor(res[:, s, :], acc[:, 2 * par + s, :], gate_row[:, par, :], ALU.mult).then_inc(acc_taken, 1)
                for s in range(SB):
                    dve.wait_ge(acc_taken, v * SB + OUT_ACC + s + 1)
                    dve.tensor_tensor(res[:, s, :], res[:, s, :], xnew[:, s, cols], ALU.add).then_inc(res_ready, 1)
                for s in range(SB):
                    dve.wait_ge(res_ready, v * SB + s + 1)
                    dve.tensor_tensor(xnew[:, s, cols], res[:, s, :], g_final_row[:, :], ALU.mult).then_inc(gained, 1)

            def out_unit(v, par):
                for i in range(TPU):
                    out_split(v, i)
                    if i == 1:
                        finish(v - 1, 1 - par)

            out_unit(1, 1)
            with dve.Fori(1, OUT_UNITS // 2) as i:
                out_unit(i * 2, 0)
                out_unit(i * 2 + 1, 1)
            v = OUT_UNITS - 1
            dve.wait_ge(gate_copied, v + 1)
            dve.wait_ge(xg_ready, v * 32 + 32)
            dve.wait_ge(res_squared, v * SB)
            dve.wait_ge(gained, v * SB)
            for s in range(SB):
                cols = slice(v * GW, D)
                dve.wait_ge(acc_done, v * SB + OUT_ACC + s + 1)
                dve.tensor_tensor(res[:, s, :], acc[:, 2 + s, :], gate_row[:, 1, :], ALU.mult).then_inc(acc_taken, 1)
                dve.wait_ge(acc_taken, v * SB + OUT_ACC + s + 1)
                dve.tensor_tensor(res[:, s, :], res[:, s, :], xnew[:, s, cols], ALU.add).then_inc(res_ready, 1)
                dve.wait_ge(res_ready, v * SB + s + 1)
                dve.tensor_tensor(xnew[:, s, cols], res[:, s, :], g_final_row[:, :], ALU.mult).then_inc(gained, 1)
                dve.wait_ge(res_squared, v * SB + s + 1)
                dve.reduce_sum(out_sum[:, s:s + 1], out_sums[:, s, :], AX.X).then_inc(tail_step, 1)
                dve.wait_ge(tail_step, 2 * s + 1)
                dve.tensor_scalar(out_sum[:, s:s + 1], out_sum[:, s:s + 1], 1.0 / D, EPS, ALU.mult, ALU.add).then_inc(tail_step, 1)
            dve.wait_ge(out_rstd_ready, 2)
            dve.wait_ge(gained, OUT_UNITS * SB)
            for lo, hi in STORES:
                dve.tensor_scalar(xnew[:, 1, lo:hi], xnew[:, 1, lo:hi], out_rstd[:, 1:2], None, ALU.mult).then_inc(scaled[1], 1)

        @block.tensor
        def _(pe):
            pe.wait_ge(ident_ready, 3)
            pe.wait_ge(vec_ready, 96)
            pe.transpose(att[:, 1, 0:2 * KC], bias_rows[:, :], ident[0:2 * KC, 0:2 * KC])
            pe.transpose(att[:, 0, 0:3 * KC], vec_rows[:, :], ident[0:3 * KC, 0:3 * KC]).then_inc(vec_turned, 1)
            for s in range(SB):
                pe.wait_ge(x_stat, 3 * (s + 1))
                for b in range(TPU):
                    n = s * TPU + b
                    if n >= 4:
                        pe.wait_ge(x_copied, n - 3)
                    for k in range(TK):
                        kc = b * TK + k
                        mm = pe.matmul(acc[:, b % 4, k * P:(k + 1) * P], x_half[:, kc * P:(kc + 1) * P], diag[:, :],
                                       start=True, stop=True)
                    mm.then_inc(x_turned, 1)
            def turned_tile(i, w, last):
                for kk in range(TK):
                    k = i * TK + kk
                    for e in range(HG):
                        pe.matmul(acc[:, e, :], w_hi[:, w, kk, e * P:(e + 1) * P], act_split[:, k, :],
                                  start=(k == 0), stop=False, skip_group_check=True)
                        mm = pe.matmul(acc[:, e, 0:S], w_lo[:, w, kk, e * P:(e + 1) * P], act_split[:, k, 0:S],
                                       start=False, stop=(k == KC - 1), skip_group_check=True)
                        if last and kk == TK - 1:
                            mm.then_inc(acc_done, 1)
                if not last:
                    mm.then_inc(tile_done, 1)

            def rows_tile(i, w, last, bank):
                for s in range(SB):
                    for kk in range(TK):
                        k = i * TK + kk
                        a_hi = act_split[:, k, s * P:(s + 1) * P]
                        a_lo = act_split[:, k, S + s * P:S + (s + 1) * P]
                        pe.matmul(acc[:, bank + s, :], a_hi, w_hi[:, w, kk, :], start=(k == 0), stop=False)
                        pe.matmul(acc[:, bank + s, :], a_hi, w_lo[:, w, kk, :], start=False, stop=False)
                        mm = pe.matmul(acc[:, bank + s, :], a_lo, w_hi[:, w, kk, :], start=False, stop=(k == KC - 1))
                    if last:
                        mm.then_inc(acc_done, 1)
                if not last:
                    mm.then_inc(tile_done, 1)

            def packed_tile(i, w, first_bank, last):
                for kk in range(TK):
                    k = i * TK + kk
                    for e in range(HG):
                        dst = acc[:, first_bank + e // 2, (e % 2) * S:(e % 2 + 1) * S]
                        w_h, w_l = (a[:, w, kk, e * P:(e + 1) * P] for a in (w_hi, w_lo))
                        pe.matmul(dst, w_h, act_split[:, k, 0:S], start=(k == 0 and e % 2 == 0), stop=False, skip_group_check=True)
                        pe.matmul(dst, w_h, act_split[:, k, S:2 * S], start=False, stop=False, skip_group_check=True)
                        mm = pe.matmul(dst, w_l, act_split[:, k, 0:S], start=False, stop=(k == KC - 1), skip_group_check=True)
                        if last and kk == TK - 1 and e % 2 == 1:
                            mm.then_inc(acc_done, 1)
                if not last:
                    mm.then_inc(tile_done, 1)

            def phase_tile(j, r):
                i, w = j - 1, r % 2
                if j < PHASES:
                    pe.wait_ge(ring_used, FIRST_ENTRIES + (j - 1) * PHASE_ENTRIES + positions("w", PHASE)[r] + 1)
                else:
                    pe.wait_ge(ring_used, LAST_BASE + positions("w", LAST)[r] + 1)
                if r == 0:
                    pe.wait_ge(split_lo, j)
                t = ORDER[r][0]
                u = r - U0
                summed = 0 <= u < NS
                if t in "qk" and not summed:
                    packed_tile(i, w, 2 * "qk".index(t), i == TPU - 1)
                    return
                for s in range(SB):
                    if summed and (j > 1 or u):
                        pe.wait_ge(part_taken, ((j - 1) * NS + u - 1) * SB + s + 1)
                    dst = att[:, (2 if summed else 0) + s, :]
                    for kk in range(TK):
                        k = i * TK + kk
                        if t == "k":
                            for e in range(2):
                                half = dst[:, e * S:(e + 1) * S]
                                w_h, w_l = (a[:, w, kk, (2 * s + e) * P:(2 * s + e + 1) * P] for a in (w_hi, w_lo))
                                pe.matmul(half, w_h, act_split[:, k, 0:S], start=(kk == 0 and e == 0), stop=False, skip_group_check=True)
                                pe.matmul(half, w_h, act_split[:, k, S:2 * S], start=False, stop=False, skip_group_check=True)
                                mm = pe.matmul(half, w_l, act_split[:, k, 0:S], start=False, stop=(kk == TK - 1), skip_group_check=True)
                            continue
                        a_hi = act_split[:, k, s * P:(s + 1) * P]
                        a_lo = act_split[:, k, S + s * P:S + (s + 1) * P]
                        begin, end = (kk == 0, kk == TK - 1) if summed else (k == 0, k == KC - 1)
                        pe.matmul(dst, a_hi, w_hi[:, w, kk, :], start=begin, stop=False)
                        pe.matmul(dst, a_hi, w_lo[:, w, kk, :], start=False, stop=False)
                        mm = pe.matmul(dst, a_lo, w_hi[:, w, kk, :], start=False, stop=end)
                    if summed:
                        mm.then_inc(part_done, 1)
                    elif i == TPU - 1:
                        mm.then_inc(acc_done, 1)
                if not summed and i < TPU - 1:
                    mm.then_inc(tile_done, 1)

            def column_sums(j):
                pe.wait_ge(ring_used, FIRST_ENTRIES + (j * PHASE_ENTRIES - 1 if j else 0))
                if j:
                    pe.wait_ge(part_taken, j * NS * SB)
                for a in range(2):
                    for k in range(TK):
                        for kk in range(2):
                            mm = pe.matmul(att[:, 3, a * TK + k:a * TK + k + 1], mod_acc[:, j % 2, kk, a, k * P:(k + 1) * P],
                                           ones[:, 0:1], start=(kk == 0), stop=(kk == 1))
                mm.then_inc(mod_summed, 1)

            column_sums(0)
            for j in range(1, PHASES):
                for r in range(len(ORDER) - 1):
                    phase_tile(j, r)
                column_sums(j)
                phase_tile(j, len(ORDER) - 1)
            for r in range(len(ORDER)):
                phase_tile(PHASES, r)

            def unit(g, kind, t, stick):
                name = UNITS[kind][t]
                if t == 0:
                    pe.wait_ge(acc_taken, acc_before(g, 0))
                elif name == "k":
                    pe.wait_ge(acc_taken, acc_before(g, 1))
                else:
                    pe.wait_ge(acc_taken, acc_before(g, t - 1) + SB)
                for i in range(TPU):
                    if kind == "final" and t == 0 and i == TPU - 2:
                        turn_probs(g - 1, stick)
                    if name == "v" and i == TPU - 1:
                        turn_y(g - 1)
                    pe.wait_ge(ring_used, g * ENTRIES[kind] + GROUP_BASE[kind] + weight_entry(kind, t, i) + 1)
                    if name in "qk":
                        turned_tile(i, i % 2, i == TPU - 1)
                    else:
                        rows_tile(i, i % 2, i == TPU - 1, 0)

            def scores(g, keys, first=False):
                if first:
                    pe.wait_ge(acc_taken, ACC_FIRST)
                    pe.wait_ge(part_taken, NS * SB * PHASES)
                else:
                    pe.wait_ge(acc_taken, acc_before(g, 2 if keys is k_t else 1))
                    pe.wait_ge(y_taken, g * HG)
                for j in range(HG):
                    pe.matmul(att[:, j, 0:P], q_t[:, j, 0:P], keys[:, j, 0:P], start=True, stop=True)
                    pe.matmul(att[:, j, P:KEYS], q_t[:, j, P:S], keys[:, j, :], start=True, stop=True).then_inc(scores_ready, 1)

            def turn_probs(G, stick):
                for j in range(HG):
                    if stick:
                        pe.wait_ge(probs_a, G * HG + j + 1)
                    else:
                        pe.wait_ge(probs_b, G * HG - SB_HEADS + j + 1)
                    for b in range(3):
                        mm = pe.transpose(att[:, j, b * P:(b + 1) * P], probs[:, j, b * P:(b + 1) * P], ident[:, :])
                    mm.then_inc(probs_turned, 1)

            def values(G):
                for j in range(HG):
                    pe.wait_ge(probs_t_ready, G * HG + j + 1)
                    pe.matmul(att[:, j, 0:VW], probs_t[:, j, 0:P], v_ones[:, 0, j, :], start=True, stop=True)
                    pe.matmul(att[:, j, VW:2 * VW], probs_t[:, j, P:2 * P], v_ones[:, 0, j, :], start=True, stop=False)
                    pe.matmul(att[:, j, VW:2 * VW], probs_t[:, j, 2 * P:KEYS], v_ones[:, 1, j, :], start=False, stop=True).then_inc(y_ready, 1)

            def turn_y(G):
                pe.wait_ge(y_normed, G * HG + HG)
                for j in range(HG):
                    for s in range(SB):
                        mm = pe.transpose(att[:, j // 2, (j % 2) * S + s * P:(j % 2) * S + (s + 1) * P], y_nat[:, j, s, :], ident[:, :])
                    mm.then_inc(y_turned, 1)

            def group(g, kind, stick):
                unit(g, kind, 0, stick)
                if kind != "final":
                    turn_probs(g - 1, stick)
                    unit(g, kind, 1, stick)
                values(g - 1)
                unit(g, kind, len(UNITS[kind]) - 1, stick)
                scores(g, k_final if kind == "final" else k_t)

            scores(0, k_t, first=True)
            pe.wait_ge(ones_set, 1)
            with pe.Fori(1, WIDE_GROUPS) as g:
                group(g, "wide", True)
            with pe.Fori(WIDE_GROUPS, GROUPS - 1) as g:
                group(g, "narrow", False)
            group(GROUPS - 1, "final", False)

            G = GROUPS - 1

            def out_unit(v, par, first=False):
                pe.wait_ge(acc_taken, OUT_ACC if first else v * SB + OUT_ACC - SB)
                for i in range(TPU):
                    if first and i == 3:
                        turn_probs(G, False)
                    if first and i == 4:
                        values(G)
                    if first and i == 6:
                        turn_y(G)
                    if i == TPU - 1:
                        if not first:
                            pe.wait_ge(gate_copied, v - 1) if not isinstance(v, int) or v > 1 else None
                        pe.matmul(att[:, 2 + par, :], ones[:, :], ada_acc[:, bass.ds(v * GW, GW)], start=True, stop=True).then_inc(gate_ready, 1)
                    pe.wait_ge(ring_used, v * TPU + OUT_BASE + i + 1)
                    if first:
                        pe.wait_ge(split_lo, TPU + i + 1)
                    rows_tile(i, i % 2, i == TPU - 1, 2 * par)

            out_unit(0, 0, first=True)
            out_unit(1, 1)
            with pe.Fori(1, OUT_UNITS // 2) as i:
                out_unit(i * 2, 0)
                out_unit(i * 2 + 1, 1)


_INS = ["x", "c", "w_ada", "b_ada", "g_norm", "w_in", "g_sb", "g_dil", "w_out", "g_final"]


def kernel(**inputs):
    import concourse.bacc as bacc
    from concourse.bass_utils import run_bass_kernel_spmd

    nc = bacc.Bacc("TRN2", target_bir_lowering=False, num_devices=1, dynamic_dma_scratch_size=1024)
    arrays, args = {}, []
    for name in _INS:
        a = np.ascontiguousarray(inputs[name])
        arrays[f"in_{name}"] = a
        args.append(nc.dram_tensor(f"in_{name}", a.shape, mybir.dt.from_np(a.dtype), kind="ExternalInput").ap())
    shape = inputs["x"].shape
    args.append(nc.dram_tensor("out", shape, F32, kind="ExternalOutput").ap())
    build(nc, *args)
    r = run_bass_kernel_spmd(nc, [arrays], core_ids=[0])
    return r.results[0]["out"]
```
